# Optimizing a Trainium2 kernel written in Bass

```python
import jax, jax.numpy as jnp
from jax import lax
import numpy as np
import jax
import jax.numpy as jnp

D_MODEL = 1024
BATCH = 1
SEQ = 256
DEPTH = 2

CHUNK = 64
HEAD_DIM = 64
ROPE_THETA = 10000.0
EPS = 1e-6
A_Q_HEADS = (D_MODEL // 2) // HEAD_DIM
A_KV_HEADS = A_Q_HEADS // 4
A_WINDOW = 128
A_PREV_CHUNKS = A_WINDOW // CHUNK
B_KEY_DIM = 128
B_VAL_DIM = 128
B_HEADS = (D_MODEL // 2) // B_VAL_DIM
B_BLOCK = 32
C_HEADS = D_MODEL // HEAD_DIM
C_PREV_CHUNKS = 8
REL_CLIP = 128
D_FF = 2816
CONV_WIDTH = 3
A_Q_DIM = A_Q_HEADS * HEAD_DIM
A_KV_DIM = A_KV_HEADS * HEAD_DIM
B_QK_DIM = B_HEADS * B_KEY_DIM
B_V_DIM = B_HEADS * B_VAL_DIM
EVEN_IN = A_Q_DIM + 2 * A_KV_DIM + 2 * B_QK_DIM + 2 * B_V_DIM
EVEN_MIX = A_Q_DIM + B_V_DIM
EVEN_SPLITS = (A_Q_DIM,
               A_Q_DIM + A_KV_DIM,
               A_Q_DIM + 2 * A_KV_DIM,
               A_Q_DIM + 2 * A_KV_DIM + B_QK_DIM,
               A_Q_DIM + 2 * A_KV_DIM + 2 * B_QK_DIM,
               A_Q_DIM + 2 * A_KV_DIM + 2 * B_QK_DIM + B_V_DIM)
C_DIM = C_HEADS * HEAD_DIM
ODD_IN = 3 * C_DIM
N_EVEN = (DEPTH + 1) // 2
N_ODD = DEPTH // 2


F32 = jnp.float32

def rms_norm(x, w):
    xf = x.astype(F32)
    y = xf * lax.rsqrt(jnp.mean(xf * xf, axis=-1, keepdims=True) + EPS)
    return (y * w.astype(F32)).astype(x.dtype)

def rope(x):
    S, D = x.shape[1], x.shape[3]
    inv_freq = ROPE_THETA ** (-jnp.arange(0, D, 2, dtype=F32) / D)
    ang = jnp.arange(S, dtype=F32)[:, None] * inv_freq[None, :]
    cos = jnp.cos(ang)[None, :, None, :]
    sin = jnp.sin(ang)[None, :, None, :]
    xf = x.astype(F32)
    x1, x2 = xf[..., : D // 2], xf[..., D // 2:]
    return jnp.concatenate([x1 * cos - x2 * sin, x2 * cos + x1 * sin], axis=-1).astype(x.dtype)

def chunk_band_attention(q, k, v, n_prev, bias, sinks):
    B, S, Hq, D = q.shape
    Hkv = k.shape[2]
    G = Hq // Hkv
    n_chunks = S // CHUNK
    pad = n_prev * CHUNK
    band = pad + CHUNK
    scale = D ** -0.5
    k_pad = jnp.pad(k, ((0, 0), (pad, 0), (0, 0), (0, 0)))
    v_pad = jnp.pad(v, ((0, 0), (pad, 0), (0, 0), (0, 0)))
    qc = jnp.moveaxis(q.reshape(B, n_chunks, CHUNK, Hkv, G, D), 1, 0)
    key_idx = jnp.arange(band)

    def one_chunk(args):
        c, q_c = args
        start = c * CHUNK
        k_c = lax.dynamic_slice_in_dim(k_pad, start, band, axis=1)
        v_c = lax.dynamic_slice_in_dim(v_pad, start, band, axis=1)
        s = jnp.einsum('bqhgd,bjhd->bhgqj', q_c, k_c).astype(F32) * scale
        if bias is not None:
            s = s + bias.reshape(Hkv, G, CHUNK, band).astype(F32)
        valid = key_idx >= pad - start
        s = jnp.where(valid, s, -jnp.inf)
        if sinks is not None:
            sk = sinks.reshape(Hkv, G).astype(F32)[None, :, :, None, None]
            m = jnp.maximum(jnp.max(s, axis=-1, keepdims=True), sk)
            p = jnp.exp(s - m)
            p = p / (jnp.sum(p, axis=-1, keepdims=True) + jnp.exp(sk - m))
        else:
            p = jax.nn.softmax(s, axis=-1)
        o = jnp.einsum('bhgqj,bjhd->bqhgd', p.astype(v.dtype), v_c)
        return o.reshape(B, CHUNK, Hq, D)

    out = lax.map(one_chunk, (jnp.arange(n_chunks), qc))
    return jnp.moveaxis(out, 0, 1).reshape(B, S, Hq, D)

def hgrn2(q, f_logit, i, g, lb, norm_w):
    B, S, H, DK = q.shape
    DV = i.shape[-1]
    N = S // B_BLOCK
    lbh = lb.reshape(H, DK).astype(F32)
    f = lbh + (1.0 - lbh) * jax.nn.sigmoid(f_logit.astype(F32))
    log_f = jnp.log(f)
    k = 1.0 - f

    def blk(t):
        return t.reshape(B, N, B_BLOCK, H, t.shape[-1])

    qf, kf, vf, lf = blk(q.astype(F32)), blk(k), blk(i.astype(F32)), blk(log_f)
    cum = jnp.cumsum(lf, axis=2)
    last = cum[:, :, -1:]
    q_dec = qf * jnp.exp(cum)
    k_dec = kf * jnp.exp(-cum)
    k_end = kf * jnp.exp(last - cum)
    blk_decay = jnp.exp(last[:, :, 0])
    causal = jnp.tril(jnp.ones((B_BLOCK, B_BLOCK), dtype=bool))
    s = jnp.einsum('bnlhd,bnmhd->bnhlm', q_dec, k_dec)
    s = jnp.where(causal, s, 0.0)
    o_intra = jnp.einsum('bnhlm,bnmhe->bnlhe', s, vf)

    def step(state, xs):
        qd, ke, vv, dec = xs
        o = jnp.einsum('blhd,bhde->blhe', qd, state)
        state = dec[..., None] * state + jnp.einsum('blhd,blhe->bhde', ke, vv)
        return state, o

    state0 = jnp.zeros((B, H, DK, DV), F32)
    xs = (jnp.moveaxis(q_dec, 1, 0), jnp.moveaxis(k_end, 1, 0),
          jnp.moveaxis(vf, 1, 0), jnp.moveaxis(blk_decay, 1, 0))
    _, o_inter = lax.scan(step, state0, xs)
    o = (o_intra + jnp.moveaxis(o_inter, 0, 1)).reshape(B, S, H, DV)
    o = o * lax.rsqrt(jnp.mean(o * o, axis=-1, keepdims=True) + EPS) * norm_w.reshape(H, DV).astype(F32)
    return (o * jax.nn.silu(g.astype(F32))).astype(i.dtype)

def even_mixer(y, w_in, w_out, sinks, lb, gnorm_w):
    B, S, _ = y.shape
    proj = y @ w_in
    qa, ka, va, qb, fb, ib, gb = jnp.split(proj, EVEN_SPLITS, axis=-1)
    qa = rope(qa.reshape(B, S, A_Q_HEADS, HEAD_DIM))
    ka = rope(ka.reshape(B, S, A_KV_HEADS, HEAD_DIM))
    va = va.reshape(B, S, A_KV_HEADS, HEAD_DIM)
    oa = chunk_band_attention(qa, ka, va, A_PREV_CHUNKS, None, sinks)
    ob = hgrn2(qb.reshape(B, S, B_HEADS, B_KEY_DIM), fb.reshape(B, S, B_HEADS, B_KEY_DIM),
               ib.reshape(B, S, B_HEADS, B_VAL_DIM), gb.reshape(B, S, B_HEADS, B_VAL_DIM),
               lb, gnorm_w)
    o = jnp.concatenate([oa.reshape(B, S, A_Q_DIM), ob.reshape(B, S, B_V_DIM)], axis=-1)
    return o @ w_out

def odd_mixer(y, w_in, w_out, rel_table):
    B, S, _ = y.shape
    proj = y @ w_in
    q, k, v = jnp.split(proj, (C_DIM, 2 * C_DIM), axis=-1)
    q = q.reshape(B, S, C_HEADS, HEAD_DIM)
    k = k.reshape(B, S, C_HEADS, HEAD_DIM)
    v = v.reshape(B, S, C_HEADS, HEAD_DIM)
    pad = C_PREV_CHUNKS * CHUNK
    band = pad + CHUNK
    rel = jnp.arange(CHUNK)[:, None] + pad - jnp.arange(band)[None, :]
    idx = jnp.clip(rel, -REL_CLIP, REL_CLIP) + REL_CLIP
    bias = rel_table[:, idx]
    o = chunk_band_attention(q, k, v, C_PREV_CHUNKS, bias, None)
    return o.reshape(B, S, C_DIM) @ w_out

def conv_ffn(y, w_up, conv_w, conv_b, w_down):
    S = y.shape[1]
    up = y @ w_up
    u, v = jnp.split(up, 2, axis=-1)
    u_pad = jnp.pad(u, ((0, 0), (CONV_WIDTH - 1, 0), (0, 0)))
    c = conv_b
    for j in range(CONV_WIDTH):
        c = c + conv_w[j] * u_pad[:, j:j + S]
    return (jax.nn.gelu(c, approximate=False) * v) @ w_down

def first_inputs(seed: int = 0) -> dict:
    key = jax.random.key(seed)
    ks = jax.random.split(key, 16)
    nrm = jax.random.normal
    x = nrm(ks[0], (BATCH, SEQ, D_MODEL), F32)
    even_w_in = nrm(ks[1], (N_EVEN, D_MODEL, EVEN_IN), F32) * D_MODEL ** -0.5
    even_w_out = nrm(ks[2], (N_EVEN, EVEN_MIX, D_MODEL), F32) * EVEN_MIX ** -0.5
    even_sinks = nrm(ks[3], (N_EVEN, A_Q_HEADS), F32) * 0.5
    hgrn_lb_logits = nrm(ks[4], (N_EVEN + 1, B_QK_DIM), F32) * 0.1
    hgrn_norm_w = 1.0 + 0.02 * nrm(ks[5], (N_EVEN, B_V_DIM), F32)
    odd_w_in = nrm(ks[6], (N_ODD, D_MODEL, ODD_IN), F32) * D_MODEL ** -0.5
    odd_w_out = nrm(ks[7], (N_ODD, C_DIM, D_MODEL), F32) * C_DIM ** -0.5
    odd_rel_bias = nrm(ks[8], (N_ODD, C_HEADS, 2 * REL_CLIP + 1), F32) * 0.1
    ffn_w_up = nrm(ks[9], (DEPTH, D_MODEL, 2 * D_FF), F32) * D_MODEL ** -0.5
    ffn_conv_w = nrm(ks[10], (DEPTH, CONV_WIDTH, D_FF), F32) * CONV_WIDTH ** -0.5
    ffn_conv_b = nrm(ks[11], (DEPTH, D_FF), F32) * 0.02
    ffn_w_down = nrm(ks[12], (DEPTH, D_FF, D_MODEL), F32) * D_FF ** -0.5
    norm_w = 1.0 + 0.02 * nrm(ks[13], (DEPTH, 4, D_MODEL), F32)
    return {"x": x, "even_w_in": even_w_in, "even_w_out": even_w_out, "even_sinks": even_sinks,
            "hgrn_lb_logits": hgrn_lb_logits, "hgrn_norm_w": hgrn_norm_w,
            "odd_w_in": odd_w_in, "odd_w_out": odd_w_out, "odd_rel_bias": odd_rel_bias,
            "ffn_w_up": ffn_w_up, "ffn_conv_w": ffn_conv_w, "ffn_conv_b": ffn_conv_b,
            "ffn_w_down": ffn_w_down, "norm_w": norm_w}

def first_block(x, even_w_in, even_w_out, even_sinks, hgrn_lb_logits, hgrn_norm_w,
              odd_w_in, odd_w_out, odd_rel_bias, ffn_w_up, ffn_conv_w, ffn_conv_b,
              ffn_w_down, norm_w):
    lb_all = jnp.cumsum(jax.nn.softmax(hgrn_lb_logits.astype(F32), axis=0), axis=0)
    h = x
    for layer in range(DEPTH):
        nw = norm_w[layer]
        j = layer // 2
        y = rms_norm(h, nw[0])
        if layer % 2 == 0:
            y = even_mixer(y, even_w_in[j], even_w_out[j], even_sinks[j], lb_all[j], hgrn_norm_w[j])
        else:
            y = odd_mixer(y, odd_w_in[j], odd_w_out[j], odd_rel_bias[j])
        h = h + rms_norm(y, nw[1])
        y = conv_ffn(rms_norm(h, nw[2]), ffn_w_up[layer], ffn_conv_w[layer], ffn_conv_b[layer], ffn_w_down[layer])
        h = h + rms_norm(y, nw[3])
    return h


DEPTH_2 = 1

MEM_LEN = 256
MOBA_HEADS = 8
MOBA_HEAD_DIM = 64
MOBA_BLOCK = 256
MOBA_TOPK = 3
FOX_HEADS = 8
FOX_HEAD_DIM = 64
MEM_HEADS = 4
MEM_HEAD_DIM = 128
Q_BLOCK = 128
ROPE_THETA_2 = 500000.0
ROPE_FRACTION_DIV = 4
N_BRANCHES = 3
D_FF_2 = ((-((-8 * D_MODEL) // 3)) + 255) // 256 * 256
NORM_EPS = 1e-6
MOBA_WIDTH = MOBA_HEADS * MOBA_HEAD_DIM
FOX_WIDTH = FOX_HEADS * FOX_HEAD_DIM
MEM_WIDTH = MEM_HEADS * MEM_HEAD_DIM
IN_SIZES = (MOBA_WIDTH,) * 3 + (FOX_WIDTH,) * 3 + (FOX_HEADS, MEM_WIDTH) + (D_MODEL,) * N_BRANCHES
D_IN = sum(IN_SIZES)


def rms_norm_2(x, gain):
    xf = x.astype(jnp.float32)
    y = xf * lax.rsqrt(jnp.mean(xf * xf, axis=-1, keepdims=True) + NORM_EPS)
    return (y * gain.astype(jnp.float32)).astype(x.dtype)

def split_heads(t, n_heads):
    b, s, _ = t.shape
    return t.reshape(b, s, n_heads, -1).transpose(0, 2, 1, 3)

def merge_heads(t):
    b, h, s, d = t.shape
    return t.transpose(0, 2, 1, 3).reshape(b, s, h * d)

def partial_rope(t):
    seq, dim = t.shape[2], t.shape[3]
    rot = dim // ROPE_FRACTION_DIV
    half = rot // 2
    inv_freq = 1.0 / (ROPE_THETA_2 ** (jnp.arange(half, dtype=jnp.float32) * 2.0 / rot))
    ang = jnp.arange(seq, dtype=jnp.float32)[:, None] * inv_freq[None, :]
    cos, sin = jnp.cos(ang), jnp.sin(ang)
    tf = t.astype(jnp.float32)
    x1, x2 = tf[..., :half], tf[..., half:rot]
    out = jnp.concatenate([x1 * cos - x2 * sin, x2 * cos + x1 * sin, tf[..., rot:]], axis=-1)
    return out.astype(t.dtype)

def moba_attention(q, k, v):
    b, h, s, d = q.shape
    scale = d ** -0.5
    n_blocks = -(-s // MOBA_BLOCK)
    pad = n_blocks * MOBA_BLOCK - s
    kp = jnp.pad(k, ((0, 0), (0, 0), (0, pad), (0, 0)))
    vp = jnp.pad(v, ((0, 0), (0, 0), (0, pad), (0, 0)))
    kb = kp.reshape(b, h, n_blocks, MOBA_BLOCK, d)
    vb = vp.reshape(b, h, n_blocks, MOBA_BLOCK, d)
    k_mean = jnp.mean(kb.astype(jnp.float32), axis=3)
    topk = min(MOBA_TOPK, n_blocks)
    b_idx = jnp.arange(b)[:, None, None, None]
    h_idx = jnp.arange(h)[None, :, None, None]
    key_off = jnp.arange(MOBA_BLOCK)
    q_off = jnp.arange(Q_BLOCK)
    block_ids = jnp.arange(n_blocks)

    def chunk(ci):
        t0 = ci * Q_BLOCK
        cur = t0 // MOBA_BLOCK
        qc = lax.dynamic_slice_in_dim(q, t0, Q_BLOCK, axis=2)
        gate = jnp.einsum('bhqd,bhnd->bhqn', qc.astype(jnp.float32), k_mean)
        gate = jnp.where(block_ids < cur, gate, -jnp.inf)
        _, sel = lax.top_k(gate, topk)
        sel_valid = sel < cur
        k_sel = kb[b_idx, h_idx, sel]
        v_sel = vb[b_idx, h_idx, sel]
        s_sel = jnp.einsum('bhqd,bhqnkd->bhqnk', qc, k_sel).astype(jnp.float32) * scale
        s_sel = jnp.where(sel_valid[..., None], s_sel, -jnp.inf)
        k_own = lax.dynamic_slice_in_dim(kp, cur * MOBA_BLOCK, MOBA_BLOCK, axis=2)
        v_own = lax.dynamic_slice_in_dim(vp, cur * MOBA_BLOCK, MOBA_BLOCK, axis=2)
        s_own = jnp.einsum('bhqd,bhkd->bhqk', qc, k_own).astype(jnp.float32) * scale
        causal = (key_off[None, :] + cur * MOBA_BLOCK) <= (q_off[:, None] + t0)
        s_own = jnp.where(causal, s_own, -jnp.inf)
        scores = jnp.concatenate([s_sel.reshape(b, h, Q_BLOCK, topk * MOBA_BLOCK), s_own], axis=-1)
        p = jax.nn.softmax(scores, axis=-1).astype(v.dtype)
        p_sel = p[..., :topk * MOBA_BLOCK].reshape(b, h, Q_BLOCK, topk, MOBA_BLOCK)
        p_own = p[..., topk * MOBA_BLOCK:]
        return (jnp.einsum('bhqnk,bhqnkd->bhqd', p_sel, v_sel)
                + jnp.einsum('bhqk,bhkd->bhqd', p_own, v_own))

    out = lax.map(chunk, jnp.arange(s // Q_BLOCK))
    return jnp.moveaxis(out, 0, 2).reshape(b, h, s, d)

def fox_attention(q, k, v, log_f):
    b, h, s, d = q.shape
    scale = d ** -0.5
    cum = jnp.cumsum(log_f, axis=-1)
    key_pos = jnp.arange(s)
    q_off = jnp.arange(Q_BLOCK)

    def chunk(ci):
        t0 = ci * Q_BLOCK
        qc = lax.dynamic_slice_in_dim(q, t0, Q_BLOCK, axis=2)
        cq = lax.dynamic_slice_in_dim(cum, t0, Q_BLOCK, axis=2)
        scores = (jnp.einsum('bhqd,bhkd->bhqk', qc, k).astype(jnp.float32) * scale
                  + cq[..., None] - cum[:, :, None, :])
        causal = key_pos[None, :] <= (q_off[:, None] + t0)
        scores = jnp.where(causal, scores, -jnp.inf)
        p = jax.nn.softmax(scores, axis=-1).astype(v.dtype)
        return jnp.einsum('bhqk,bhkd->bhqd', p, v)

    out = lax.map(chunk, jnp.arange(s // Q_BLOCK))
    return jnp.moveaxis(out, 0, 2).reshape(b, h, s, d)

def memory_attention(q, mk, mv):
    scale = q.shape[-1] ** -0.5
    scores = jnp.einsum('bhsd,bhmd->bhsm', q, mk).astype(jnp.float32) * scale
    p = jax.nn.softmax(scores, axis=-1).astype(mv.dtype)
    return jnp.einsum('bhsm,bhmd->bhsd', p, mv)

def second_inputs(seed: int = 0) -> dict:
    key = jax.random.key(seed)
    ks = jax.random.split(key, 24)
    L = DEPTH_2

    def normal(k, shape, scale):
        return jax.random.normal(k, shape, jnp.float32) * scale

    def gain(k, shape):
        return 1.0 + 0.1 * jax.random.normal(k, shape, jnp.float32)

    return {
        "x": normal(ks[0], (BATCH, SEQ, D_MODEL), 1.0),
        "mem": normal(ks[1], (BATCH, MEM_LEN, D_MODEL), 1.0),
        "g_mix": gain(ks[2], (L, D_MODEL)),
        "w_in": normal(ks[3], (L, D_MODEL, D_IN), D_MODEL ** -0.5),
        "b_forget": 4.0 + 0.5 * jax.random.normal(ks[4], (L, FOX_HEADS), jnp.float32),
        "g_q_moba": gain(ks[5], (L, MOBA_HEAD_DIM)),
        "g_k_moba": gain(ks[6], (L, MOBA_HEAD_DIM)),
        "g_q_fox": gain(ks[7], (L, FOX_HEAD_DIM)),
        "g_k_fox": gain(ks[8], (L, FOX_HEAD_DIM)),
        "g_q_mem": gain(ks[9], (L, MEM_HEAD_DIM)),
        "g_k_mem": gain(ks[10], (L, MEM_HEAD_DIM)),
        "g_mem": gain(ks[11], (L, D_MODEL)),
        "w_mem_kv": normal(ks[12], (L, D_MODEL, 2 * MEM_WIDTH), D_MODEL ** -0.5),
        "w_br_moba": normal(ks[13], (L, MOBA_WIDTH, D_MODEL), MOBA_WIDTH ** -0.5),
        "w_br_fox": normal(ks[14], (L, FOX_WIDTH, D_MODEL), FOX_WIDTH ** -0.5),
        "w_br_mem": normal(ks[15], (L, MEM_WIDTH, D_MODEL), MEM_WIDTH ** -0.5),
        "w_out": normal(ks[16], (L, D_MODEL, D_MODEL), D_MODEL ** -0.5),
        "g_ffn": gain(ks[17], (L, D_MODEL)),
        "w_gate": normal(ks[18], (L, D_MODEL, D_FF_2), D_MODEL ** -0.5),
        "w_up": normal(ks[19], (L, D_MODEL, D_FF_2), D_MODEL ** -0.5),
        "w_down": normal(ks[20], (L, D_FF_2, D_MODEL), D_FF_2 ** -0.5),
    }

def second_block(x, mem, g_mix, w_in, b_forget, g_q_moba, g_k_moba, g_q_fox, g_k_fox, g_q_mem, g_k_mem,
              g_mem, w_mem_kv, w_br_moba, w_br_fox, w_br_mem, w_out, g_ffn, w_gate, w_up, w_down):
    split_points = np.cumsum(IN_SIZES)[:-1].tolist()
    for layer in range(DEPTH_2):
        h = rms_norm_2(x, g_mix[layer])
        proj = h @ w_in[layer]
        (q_m, k_m, v_m, q_f, k_f, v_f, f_logit, q_c, a_m, a_f, a_c) = jnp.split(proj, split_points, axis=-1)

        q_m = partial_rope(rms_norm_2(split_heads(q_m, MOBA_HEADS), g_q_moba[layer]))
        k_m = partial_rope(rms_norm_2(split_heads(k_m, MOBA_HEADS), g_k_moba[layer]))
        y_m = moba_attention(q_m, k_m, split_heads(v_m, MOBA_HEADS))

        log_f = jax.nn.log_sigmoid(f_logit.astype(jnp.float32)
                                   + b_forget[layer].astype(jnp.float32)).transpose(0, 2, 1)
        q_f = rms_norm_2(split_heads(q_f, FOX_HEADS), g_q_fox[layer])
        k_f = rms_norm_2(split_heads(k_f, FOX_HEADS), g_k_fox[layer])
        y_f = fox_attention(q_f, k_f, split_heads(v_f, FOX_HEADS), log_f)

        mkv = rms_norm_2(mem, g_mem[layer]) @ w_mem_kv[layer]
        mk, mv = jnp.split(mkv, 2, axis=-1)
        mk = rms_norm_2(split_heads(mk, MEM_HEADS), g_k_mem[layer])
        q_c = rms_norm_2(split_heads(q_c, MEM_HEADS), g_q_mem[layer])
        y_c = memory_attention(q_c, mk, split_heads(mv, MEM_HEADS))

        merged = (jax.nn.sigmoid(a_m) * (merge_heads(y_m) @ w_br_moba[layer])
                  + jax.nn.sigmoid(a_f) * (merge_heads(y_f) @ w_br_fox[layer])
                  + jax.nn.sigmoid(a_c) * (merge_heads(y_c) @ w_br_mem[layer]))
        x = x + merged @ w_out[layer]

        h2 = rms_norm_2(x, g_ffn[layer])
        x = x + (jax.nn.silu(h2 @ w_gate[layer]) * (h2 @ w_up[layer])) @ w_down[layer]
    return x


def setup_inputs(seed=0):
    out = dict(first_inputs(seed))
    for name, value in second_inputs(seed + 1).items():
        if name != "x":
            out[name + "_2"] = value
    return out


def reference(
    x, even_w_in, even_w_out, even_sinks, hgrn_lb_logits, hgrn_norm_w, odd_w_in, odd_w_out,
    odd_rel_bias, ffn_w_up, ffn_conv_w, ffn_conv_b, ffn_w_down, norm_w, mem_2, g_mix_2, w_in_2,
    b_forget_2, g_q_moba_2, g_k_moba_2, g_q_fox_2, g_k_fox_2, g_q_mem_2, g_k_mem_2, g_mem_2,
    w_mem_kv_2, w_br_moba_2, w_br_fox_2, w_br_mem_2, w_out_2, g_ffn_2, w_gate_2, w_up_2,
    w_down_2,
):
    x = first_block(
        x, even_w_in, even_w_out, even_sinks, hgrn_lb_logits, hgrn_norm_w, odd_w_in, odd_w_out,
        odd_rel_bias, ffn_w_up, ffn_conv_w, ffn_conv_b, ffn_w_down, norm_w,
    )
    return second_block(
        x, mem_2, g_mix_2, w_in_2, b_forget_2, g_q_moba_2, g_k_moba_2, g_q_fox_2, g_k_fox_2,
        g_q_mem_2, g_k_mem_2, g_mem_2, w_mem_kv_2, w_br_moba_2, w_br_fox_2, w_br_mem_2, w_out_2,
        g_ffn_2, w_gate_2, w_up_2, w_down_2,
    )


_drawn_inputs = setup_inputs


def setup_inputs(seed=0):
    import zlib

    import numpy as np

    out = dict(_drawn_inputs(seed))
    spreads = {}
    factors = {'even_sinks': 8.0,
     'hgrn_norm_w': 2.735,
     'ffn_conv_b': 3.299,
     'g_mix_2': 3.317,
     'b_forget_2': 40.728,
     'g_q_moba_2': 8.0,
     'g_k_moba_2': 8.0,
     'g_q_fox_2': 8.0,
     'g_k_fox_2': 8.0,
     'g_q_mem_2': 8.0,
     'g_k_mem_2': 8.0,
     'g_mem_2': 8.0,
     'g_ffn_2': 4.08}
    for name, (base, spread) in spreads.items():
        noise = np.random.default_rng([zlib.crc32(name.encode()), seed]).standard_normal(out[name].shape)
        drawn = base * np.exp(spread * noise) if base else spread * noise
        out[name] = jnp.asarray(drawn.astype(out[name].dtype))
    for name, factor in factors.items():
        out[name] = (out[name] * factor).astype(out[name].dtype)
    return out
```

```python
from contextlib import ExitStack

import numpy as np

import concourse.bass as bass
from concourse import mybir

F32 = mybir.dt.float32
F32R = mybir.dt.float32r
U32 = mybir.dt.uint32
ALU = mybir.AluOpType
ACT = mybir.ActivationFunctionType
AX = mybir.AxisListType

P = 128
S = 256
NT = S // P
D = 1024
KD = D // P
FF = 2816
KF = FF // P
HD = 64
EPS = 1e-6
MASKED = -3.0e38
CHUNK = 64
BLK = 32
NBLK = S // BLK
HB = 4
REL = 128

UNIT = 2048
RAW = 4
SPLIT = 2

STREAM = [
    ("mem_kv", 4, 2, 1024),
    ("even_a", 4, 2, 768), ("even_qf", 4, 8, 256), ("even_ig", 4, 2, 1024), ("even_out", 4, 2, 1024),
    ("up0", 22, 8, 256), ("down0", 11, 2, 1024),
    ("odd_q", 4, 2, 1024), ("odd_k", 4, 2, 1024), ("odd_v", 4, 2, 1024), ("odd_out", 4, 2, 1024),
    ("up1", 22, 8, 256), ("down1", 11, 2, 1024),
    ("moba_qk", 4, 2, 1024), ("both_v", 4, 2, 1024), ("fox_qk", 4, 2, 1024), ("mem_q", 3, 3, 520),
    ("gates", 12, 8, 256), ("branches", 6, 4, 512), ("merge_out", 4, 2, 1024),
    ("up2", 22, 8, 256), ("down2", 11, 2, 1024),
]
FIRST, COUNT, WIDTH, NK, COLS = {}, {}, [], {}, {}
for _name, _n, _k, _c in STREAM:
    FIRST[_name], COUNT[_name], NK[_name], COLS[_name] = len(WIDTH), _n, _k, _c
    WIDTH += [_k * _c] * _n
WIDTH[FIRST["mem_q"] + 2] = 2 * 520
UNITS = len(WIDTH)


def last(name):
    return FIRST[name] + COUNT[name]


GAINS = ["g_mem", "n00", "n01", "n02", "n03", "n10", "n11", "n12", "n13", "g_mix", "g_ffn"]


def constants():
    f = np.float32
    tok = np.arange(S, dtype=f)[:, None]
    inv = f(10000.0) ** (-np.arange(0, HD, 2, dtype=f) / f(HD))
    ang = tok * inv[None, :]
    inv2 = f(1.0) / (f(500000.0) ** (np.arange(8, dtype=f) * f(2.0) / f(16)))
    ang2 = tok * inv2[None, :]

    def by_tile(a):
        return a.reshape(NT, P, -1).transpose(1, 0, 2).reshape(P, -1)

    rope_a = np.concatenate([by_tile(np.cos(ang)), by_tile(np.sin(ang)), by_tile(-np.sin(ang))], 1)
    rope_m = np.concatenate([by_tile(np.cos(ang2)), by_tile(np.sin(ang2)), by_tile(-np.sin(ang2))], 1)
    q = np.arange(P)[:, None]
    k = np.arange(S)[None, :]

    def scores_mask(ok):
        return np.concatenate([np.where(ok(q, k[:, :P]), 0, MASKED), np.where(ok(q + P, k), 0, MASKED)], 1)

    window = scores_mask(lambda a, b: (b // CHUNK <= a // CHUNK) & (b // CHUNK >= a // CHUNK - 2))
    causal = scores_mask(lambda a, b: b <= a)
    m, l = np.arange(P)[:, None], np.arange(P)[None, :]
    block_causal = ((m // BLK == l // BLK) & (m <= l)).astype(np.uint32)
    keep = np.ones((P, S), f)
    keep[:, ::BLK] = 0
    pick = np.zeros((P, 8, P), f)
    for h in range(8):
        pick[h, h], pick[64 + h, h] = 1, 1
    return {
        "c_ident": np.eye(P, dtype=f), "c_rope_a": rope_a.astype(f), "c_rope_m": rope_m.astype(f),
        "c_window": window.astype(f), "c_causal": causal.astype(f), "c_block": block_causal,
        "c_keep": keep, "c_pick": pick.reshape(P, 8 * P),
    }


def lay_out(a):
    def rows(w, cols, k_of_unit):
        w = w[:, cols].reshape(-1, P, w[:, cols].shape[1])
        out = []
        for k0 in range(0, w.shape[0], k_of_unit):
            out.append(w[k0:k0 + k_of_unit].transpose(1, 0, 2).reshape(P, -1))
        return out

    def columns(w, groups):
        return [w[:, g].reshape(-1, P, len(g)).transpose(1, 0, 2).reshape(P, -1) for g in groups]

    r = np.arange
    pairs = [r(256 * j, 256 * j + 256) for j in range(4)]
    two = [np.concatenate([r(P * j, P * j + P), FF + r(P * j, P * j + P)]) for j in range(KF)]
    even, odd, w2 = a["even_w_in"][0], a["odd_w_in"][0], a["w_in_2"][0]
    u = rows(a["w_mem_kv_2"][0], r(1024), 2)
    heads = np.concatenate([r(HD * x, HD * x + HD) for p in range(4) for x in (p, 4 + p)] + [r(512, 768)])
    u += rows(even, heads, 2) + columns(even, [768 + g for g in pairs]) + rows(even, r(1792, 2816), 2)
    u += rows(a["even_w_out"][0], r(D), 2)
    u += columns(a["ffn_w_up"][0], two) + rows(a["ffn_w_down"][0], r(D), 2)
    for c in range(3):
        u += rows(odd, r(1024 * c, 1024 * c + 1024), 2)
    u += rows(a["odd_w_out"][0], r(D), 2)
    u += columns(a["ffn_w_up"][1], two) + rows(a["ffn_w_down"][1], r(D), 2)
    u += rows(w2, r(1024), 2) + rows(w2, np.concatenate([r(1024, 1536), r(2560, 3072)]), 2)
    u += rows(w2, r(1536, 2560), 2) + rows(w2, r(3072, 3592), 3)
    u += columns(w2, [3592 + r(256 * j, 256 * j + 256) for j in range(12)])
    for name in ("w_br_moba_2", "w_br_fox_2", "w_br_mem_2"):
        u += columns(a[name][0], [r(512), r(512, 1024)])
    u += rows(a["w_out_2"][0], r(D), 2)
    gate_up = np.concatenate([a["w_gate_2"][0], a["w_up_2"][0]], 1)
    u += columns(gate_up, two) + rows(a["w_down_2"][0], r(D), 2)
    weights = np.zeros((UNITS, P, UNIT), np.float32)
    for n, x in enumerate(u):
        weights[n, :, :x.shape[1]] = x
    nw = a["norm_w"]
    gains = np.stack([a["g_mem_2"][0], *nw[0], *nw[1], a["g_mix_2"][0], a["g_ffn_2"][0]])
    conv = np.concatenate([a["ffn_conv_w"], a["ffn_conv_b"][:, None]], 1)
    conv = conv.reshape(2, 4, KF, P).transpose(3, 0, 2, 1).reshape(P, 2 * KF * 4)
    head_gains = np.concatenate([a[x][0] for x in (
        "g_q_moba_2", "g_k_moba_2", "g_q_fox_2", "g_k_fox_2", "g_q_mem_2", "g_k_mem_2")])[None]
    rows_in = np.concatenate([a["even_sinks"][0], a["b_forget_2"][0]])[None]
    lb = a["hgrn_lb_logits"].reshape(2, HB, P).transpose(2, 0, 1).reshape(P, 2 * HB)
    table = np.pad(a["odd_rel_bias"][0][:, ::-1], ((0, 0), (127, 128)), mode="edge")
    table = np.stack([table[:, P - 1 - q:P - 1 - q + S] for q in range(P)], 1)
    return {
        "weights": weights, "gains": gains, "conv": conv, "head_gains": head_gains, "rows_in": rows_in,
        "lb": lb, "hgrn_w": a["hgrn_norm_w"], "rel": table, "x": a["x"][0], "mem": a["mem_2"][0],
    }


def build(nc, dram, out):
    with ExitStack() as ctx:
        def sb(name, shape, dt=F32, stack=ctx):
            return stack.enter_context(nc.sbuf_tensor(name, [P, *shape], dt))

        sems = {}

        def sem(name):
            sems[name] = ctx.enter_context(nc.semaphore(name))
            return sems[name]

        raw = sb("raw", [RAW, UNIT])
        hi = sb("hi", [SPLIT, UNIT], F32R)
        lo = sb("lo", [SPLIT, UNIT], F32R)
        h = sb("h", [NT, D])
        y_hi = sb("y_hi", [KD, S], F32R)
        y_lo = sb("y_lo", [KD, S], F32R)
        gain = sb("gain", [2, D])
        xhat = sb("xhat", [NT, D])
        mk_t = sb("mk_t", [4, S])
        mv = sb("mv", [NT, 512])
        sc = sb("sc", [2, 512])
        pr = sb("pr", [2, 512])
        pt = sb("pt", [2, 512])
        ident = sb("ident", [P])
        rope_a = sb("rope_a", [3, NT, 32])
        rope_m = sb("rope_m", [3, NT, 8])
        causal = sb("causal", [384])
        block_causal = sb("block_causal", [P], U32)
        ones = sb("ones", [S])
        conv = sb("conv", [2, KF, 4])
        head_gain = sb("head_gain", [512])
        rows_in = sb("rows_in", [16])
        lb_in = sb("lb_in", [2, HB])
        lb = sb("lb", [2, HB])
        lb_d = sb("lb_d", [HB])
        half = sb("half", [16])
        ss = sb("ss", [2, 2])
        ms = sb("ms", [2, 2])
        rstd = sb("rstd", [2, 2])
        hs = sb("hs", [2, 16])
        hm = sb("hm", [2, 16])
        hr = sb("hr", [2, 16])
        top = sb("top", [20, 2])
        neg = sb("neg", [20, 2])
        tot = sb("tot", [20, 2])
        rec = sb("rec", [20, 2])
        snk = sb("snk", [8, 2])
        esnk = sb("esnk", [8, 2])
        fz = sb("fz", [5, NT, 8])

        nlf = sb("nlf", [NT, P])
        ncum = sb("ncum", [S])
        pick = sb("pick", [8, P])

        with ExitStack() as r:
            h_hi = sb("h_hi", [KF, S], F32R, r)
            h_lo = sb("h_lo", [KF, S], F32R, r)
            gate = sb("gate", [24, S], F32, r)
        with ExitStack() as r:
            q_t = sb("q_t0", [4, S], F32, r)
            k_t = sb("k_t0", [S], F32, r)
            qk = sb("qk0", [NT, 640], F32, r)
            rot = sb("rot0", [640], F32, r)
            va = sb("va", [NT, P], F32, r)
            mk = sb("mk", [NT, 512], F32, r)
            hq = sb("hq", [HB, S], F32, r)
            hf = sb("hf", [HB, S], F32, r)
            hk = sb("hk", [HB, S], F32, r)
            hc = sb("hc", [HB, S], F32, r)
            he = sb("he", [HB, S], F32, r)
            hd = sb("hd", [HB, S], F32, r)
            kend = sb("kend", [NT, 512], F32, r)
            hv = sb("hv", [NT, 512], F32, r)
            hg = sb("hg", [NT, 512], F32, r)
            s_t = sb("s_t", [NT, HB, P], F32, r)
            state_own = sb("state_own", [3, HB, P], F32, r)
            hw = sb("hw", [512], F32, r)
            window = sb("window", [384], F32, r)
            keep = sb("keep", [S], F32, r)
        with ExitStack() as r:
            q1 = sb("q1", [NT, D], F32, r)
            k1 = sb("k1", [NT, D], F32, r)
            v1 = sb("v1", [NT, D], F32, r)
            q1_t = sb("q1_t", [8, S], F32, r)
            k1_t = sb("k1_t", [8, S], F32, r)
            bias = sb("bias", [2, S], F32, r)
        mem_x = k1
        with ExitStack() as r:
            qkm = sb("qkm", [NT, D], F32, r)
            qkf = sb("qkf", [NT, D], F32, r)
            v2 = sb("v2", [NT, D], F32, r)
            qkm_t = sb("qkm_t", [8, S], F32, r)
            qkf_t = sb("qkf_t", [8, S], F32, r)
            qc = sb("qc", [NT, 512], F32, r)
        ps = ctx.enter_context(nc.psum_tensor("ps", [P, 8, 512], F32))
        state = ([hf[:, 2 * i:2 * i + 2, :].rearrange("p a b -> p (a b)") for i in range(2)]
                 + [hk[:, 2 * i:2 * i + 2, :].rearrange("p a b -> p (a b)") for i in range(2)]
                 + [state_own[:, i].rearrange("p a b -> p (a b)") for i in range(3)])
        state = [s.rearrange("p (h e) -> p h e", h=HB) for s in state]
        qc_t = xhat[:, 0, :].rearrange("p (a b) -> p a b", a=4)
        m_sum = xhat[:, :, :].rearrange("p t n -> p (t n)").rearrange("p (k s) -> p k s", s=S)

        raw_in = [sem(f"raw_in{i}") for i in range(RAW)]
        const_in, ident_in = sem("const_in"), sem("ident_in")
        x_in, mem_in = sem("x_in"), sem("mem_in")
        gain_in = [sem("gain_in0"), sem("gain_in1")]
        bias_in = [sem("bias_in0"), sem("bias_in1")]
        out_in = sem("out_in")
        hi_done, lo_done = sem("hi_done"), sem("lo_done")
        unit_used = sem("unit_used")
        set_up = sem("set_up")
        squared, scaled_ms, rooted = sem("squared"), sem("scaled_ms"), sem("rooted")
        normed, post_mul, resid = sem("normed"), sem("post_mul"), sem("resid")
        turned, y_hi_done, y_lo_done = sem("turned"), sem("y_hi_done"), sem("y_lo_done")
        head_sq, head_sum, head_ms, head_root = sem("head_sq"), sem("head_sum"), sem("head_ms"), sem("head_root")
        dve_link, act_link = sem("dve_link"), sem("act_link")
        scored, row_max, maxed, powed = sem("scored"), sem("row_max"), sem("maxed"), sem("powed")
        probs_turned, probs_copied, mixed = sem("probs_turned"), sem("probs_copied"), sem("mixed")
        attended = sem("attended")
        conv_begun, conv_done, glued = sem("conv_begun"), sem("conv_done"), sem("glued")
        hmul, h_hi_done, h_lo_done = sem("hmul"), sem("h_hi_done"), sem("h_lo_done")
        mk_copied, mv_copied, hg_evac = sem("mk_copied"), sem("mv_copied"), sem("hg_evac")
        mk_ready, mk_turned, mk_evac = sem("mk_ready"), sem("mk_turned"), sem("mk_evac")
        dve_sink, act_sink = sem("dve_sink"), sem("act_sink")
        roped, a_turned, a_evac = sem("roped"), sem("a_turned"), sem("a_evac")
        lb_sub, lb_sig, lb_done = sem("lb_sub"), sem("lb_sig"), sem("lb_done")
        qf_evac, f_done, ln_done, cum_done = sem("qf_evac"), sem("f_done"), sem("ln_done"), sem("cum_done")
        exp_done, last_done, exp3_done, dec_done = sem("exp_done"), sem("last_done"), sem("exp3_done"), sem("dec_done")
        hv_evac, gated = sem("hv_evac"), sem("gated")
        kend_turned, kend_evac, st_made, st_evac = sem("kend_turned"), sem("kend_evac"), sem("st_made"), sem("st_evac")
        kv_made, stated, o_made, hgrn_out = sem("kv_made"), sem("stated"), sem("o_made"), sem("hgrn_out")
        q_evac, k_evac, v_evac, qk_turned, qk_evac = (sem(x) for x in ("q_evac", "k_evac", "v_evac", "qk_turned", "qk_evac"))
        m_evac, v2_evac, f_evac, c_evac = sem("m_evac"), sem("v2_evac"), sem("f_evac"), sem("c_evac")
        m_ready, f_ready, c_ready, nlf_ready = sem("m_ready"), sem("f_ready"), sem("c_ready"), sem("nlf_ready")
        forget, forget_e, forget_l = sem("forget"), sem("forget_e"), sem("forget_l")
        heads_turned, heads_evac = sem("heads_turned"), sem("heads_evac")
        k_copied, ncum_done, z_done = sem("k_copied"), sem("ncum_done"), sem("z_done")
        gate_evac, gate_sig = sem("gate_evac"), sem("gate_sig")
        br_turned, br_hi, br_lo, br_used = sem("br_turned"), sem("br_hi"), sem("br_lo"), sem("br_used")
        br_sum, merged_hi, merged_lo = sem("br_sum"), sem("merged_hi"), sem("merged_lo")

        block = ctx.enter_context(nc.Block())

        ATT = {"a": (0, 8, HD), "c": (8, 16, HD), "m": (24, 8, HD), "f": (32, 8, HD), "x": (40, 4, P)}
        COLUMN = {"a": 0, "c": 0, "m": 0, "f": 8, "x": 16}
        ATTENDED = {"a": 0, "c": 2, "m": 4, "f": 6, "x": 8}

        def third_heads(k):
            n = 2 * k
            return [("m", n), ("m", n + 1)] if n < 8 else [("f", n - 8), ("f", n - 7)] if n < 16 else [("x", n - 16), ("x", n - 15)]

        def branch_y(part, b, t):
            if b == 2:
                return (h_hi, h_lo)[part][:, 16:20, t * P:(t + 1) * P]
            return (y_hi, y_lo)[part][:, 4 * b:4 * b + 4, t * P:(t + 1) * P]

        junk = [sc, pr]

        def whole(tile):
            return tile[:, :, :].rearrange("p a b -> p (a b)")

        def bank(b):
            return ps[:, b, :]

        def two_banks(b):
            return ps[:, b:b + 2, :].rearrange("p a b -> p (a b)")

        def split4(ap):
            return ap.rearrange("p (a b) -> p a b", a=4)

        def token_half(y, kh, t):
            return y[:, 4 * kh:4 * kh + 4, t * P:(t + 1) * P]

        @block.sync
        def _(sp):
            sp.dma_start(h[:, :, :], dram["x"].rearrange("(t p) d -> p t d", p=P)).then_inc(x_in, 16)
            sp.dma_start(ident[:, :], dram["c_ident"]).then_inc(ident_in, 16)
            for n in range(RAW):
                sp.dma_start(raw[:, n, :], dram["weights"][n]).then_inc(raw_in[n], 16)
            with sp.Fori(0, UNITS // RAW - 1) as i:
                for s in range(RAW):
                    sp.wait_ge(lo_done, RAW * i + s + 1)
                    sp.dma_start(raw[:, s, :], dram["weights"][RAW * i + (RAW + s)]).then_inc(raw_in[s], 16)
            for t in range(NT):
                sp.wait_ge(resid, 10 + t + 1)
                sp.dma_start(out[t * P:(t + 1) * P, :], h[:, t, :]).then_inc(out_in, 16)
            sp.wait_ge(out_in, 32)

        @block.gpsimd
        def _(pool):
            pool.dma_start(mem_x[:, :, :], dram["mem"].rearrange("(t p) d -> p t d", p=P)).then_inc(mem_in, 16)

            def gain_load(g):
                pool.dma_start(gain[:, g % 2, :], dram["gains"][g:g + 1, :].partition_broadcast(P)).then_inc(gain_in[g % 2], 16)

            gain_load(0)
            gain_load(1)
            loads = [
                (rope_a[:, :, :, :].rearrange("p a t f -> p (a t f)"), dram["c_rope_a"]),
                (rope_m[:, :, :, :].rearrange("p a t f -> p (a t f)"), dram["c_rope_m"]),
                (window[:, :], dram["c_window"]), (causal[:, :], dram["c_causal"]),
                (block_causal[:, :], dram["c_block"]), (keep[:, :], dram["c_keep"]),
                (pick[:, :, :].rearrange("p a b -> p (a b)"), dram["c_pick"]),
                (conv[:, :, :, :].rearrange("p a b c -> p (a b c)"), dram["conv"]),
                (head_gain[:, :], dram["head_gains"].partition_broadcast(P)),
                (rows_in[:, :], dram["rows_in"].partition_broadcast(P)),
                (lb_in[:, :, :].rearrange("p a b -> p (a b)"), dram["lb"]),
                (hw[:, :], dram["hgrn_w"].partition_broadcast(P)),
            ]
            for dst, src in loads:
                pool.dma_start(dst, src).then_inc(const_in, 16)
            pool.memset(half[:, :], -0.5).then_inc(set_up, 1)
            pool.memset(ones[:, :], 1.0).then_inc(set_up, 1)
            pool.memset(s_t[:, :, :, :], 0.0).then_inc(set_up, 1)
            pool.memset(nlf[:, :, :], 0.0).then_inc(set_up, 1)

            def root(g):
                for t in range(NT):
                    n = 2 * g + t + 1
                    if n == 1:
                        pool.wait_ge(set_up, 1)
                    pool.wait_ge(squared, n)
                    pool.tensor_scalar(ms[:, g % 2, t:t + 1], ss[:, g % 2, t:t + 1], 1.0 / D, EPS, ALU.mult, ALU.add).then_inc(scaled_ms, 1)
                    pool.wait_ge(scaled_ms, n)
                    pool.tensor_tensor(rstd[:, g % 2, t:t + 1], ms[:, g % 2, t:t + 1], half[:, 0:1], ALU.pow).then_inc(rooted, 1)

            def head_roots(i, nh, d):
                pool.wait_ge(head_sum, i + 1)
                pool.tensor_scalar(hm[:, i % 2, :nh], hs[:, i % 2, :nh], 1.0 / d, EPS, ALU.mult, ALU.add).then_inc(head_ms, 1)
                pool.wait_ge(head_ms, i + 1)
                pool.tensor_tensor(hr[:, i % 2, :nh], hm[:, i % 2, :nh], half[:, :nh], ALU.pow).then_inc(head_root, 1)

            root(0)
            root(1)
            pool.wait_ge(normed, 2)
            gain_load(2)
            pool.wait_ge(normed, 4)
            gain_load(3)
            for i in range(2):
                head_roots(i, 4, P)
            pool.wait_ge(const_in, 16 * 12)
            for t in range(NT):
                pool.wait_ge(hg_evac, t + 1)
                pool.tensor_tensor(hg[:, t, :], hg[:, t, :], hw[:, :], ALU.mult).then_inc(gated, 1)
            for i in range(2, 4):
                head_roots(i, 4, P)
            root(2)
            pool.wait_ge(post_mul, 2)
            gain_load(4)
            root(3)
            pool.wait_ge(normed, 6)
            gain_load(5)
            root(4)
            pool.wait_ge(post_mul, 4)
            gain_load(6)
            root(5)
            pool.wait_ge(normed, 8)
            gain_load(7)
            pool.wait_ge(q_evac, 2)
            for b in range(2):
                pool.memset(bias[0:CHUNK, b, S - CHUNK:S], MASKED).then_inc(set_up, 1)
            for hh in range(16):
                if hh >= 2:
                    pool.wait_ge(row_max, ATT["c"][0] + hh - 1)
                for q0, width in ((0, S - CHUNK), (CHUNK, S)):
                    pool.dma_start(bias[q0:q0 + CHUNK, hh % 2, 0:width], dram["rel"][hh, q0:q0 + CHUNK, 0:width]).then_inc(bias_in[hh % 2], 16)
            root(6)
            pool.wait_ge(post_mul, 6)
            gain_load(8)
            root(7)
            pool.wait_ge(normed, 10)
            gain_load(9)
            root(8)
            pool.wait_ge(post_mul, 8)
            gain_load(10)
            root(9)
            for i in (4, 5, 6, 7):
                head_roots(i, 16, HD)
            for i in (8, 9):
                head_roots(i, 4, P)
            root(10)

        @block.scalar
        def _(act):
            done = [0]

            def round_unit(n, s=None, q=None, w=None):
                s, q = (n % RAW, n // RAW) if s is None else (s, q)
                act.wait_ge(raw_in[s], 16 * (q + 1))
                if not (type(n) is int and n < SPLIT):
                    act.wait_ge(unit_used, n - 1)
                w = WIDTH[n] if w is None else w
                act.activation(hi[:, s % SPLIT, :w], raw[:, s, :w], ACT.Copy).then_inc(hi_done, 1)

            def units(upto):
                while done[0] < upto:
                    round_unit(done[0])
                    done[0] += 1

            def square(g, src, ready, count):
                for t in range(NT):
                    if g:
                        act.wait_ge(squared, 2 * g)
                    act.wait_ge(ready, count[t])
                    act.activation(whole(junk[t]), src(t), ACT.Square, accum_out=ss[:, g % 2, t:t + 1]).then_inc(squared, 1)

            def turned_hi(stage, base, dst):
                for t in range(NT):
                    for kh in range(2):
                        act.wait_ge(turned, 4 * stage + 2 * t + kh + 1)
                        act.activation(token_half(dst, kh, t), split4(bank(base + 2 * t + kh)), ACT.Copy).then_inc(y_hi_done, 1)

            def head_square(i, src, nh, d):
                if i >= 2:
                    act.wait_ge(head_sum, i - 1)
                act.activation(whole(junk[i % 2])[:, :nh * d].rearrange("p (a b) -> p a b", a=nh), src, ACT.Square).then_inc(head_sq, 1)

            def exps(stage, hh):
                a, col = ATT[stage][0] + hh, COLUMN[stage] + hh
                act.wait_ge(maxed, a + 1)
                if a >= 2:
                    act.wait_ge(probs_turned, a - 1)
                for t in range(NT):
                    c = slice(256 * t, 256 * t + 256) if stage == "x" else slice(P * t, P + 256 * t)
                    src = ps[:, a % 2, c] if stage == "x" else sc[:, a % 2, c]
                    e = act.activation(pr[:, a % 2, c], src, ACT.Exp, bias=neg[:, col, t:t + 1], accum_out=tot[:, col, t:t + 1])
                e.then_inc(powed, 1)

            def feed_forward(layer):
                up = FIRST[f"up{layer}"]
                J0 = KF * layer

                def begin(j, n, s):
                    act.wait_ge(unit_used, n + 1)
                    if layer < 2:
                        act.activation(sc[:, s % 2, :S], ps[:, s % 4, :S], ACT.Identity, scale=conv[:, layer, j, 2:3],
                                       bias=conv[:, layer, j, 3:4]).then_inc(conv_begun, 1)

                def copy(j):
                    act.wait_ge(hmul, J0 + j + 1)
                    act.activation(h_hi[:, j, :], pt[:, j % 2, :S], ACT.Copy).then_inc(h_hi_done, 1)

                for j in range(KF):
                    begin(j, up + j, j)
                    if j >= 1:
                        copy(j - 1)
                    units(up + j + 3)
                    if layer < 2:
                        act.wait_ge(conv_done, J0 + j + 1)
                        act.activation(pr[:, j % 2, :S], sc[:, j % 2, :S], ACT.Gelu).then_inc(glued, 1)
                    else:
                        act.activation(pr[:, j % 2, :S], ps[:, j % 4, :S], ACT.Silu).then_inc(glued, 1)
                copy(KF - 1)
                units(last(f"down{layer}") + (2 if layer < 2 else 0))

            units(2)
            square(0, lambda t: mem_x[:, t, :], mem_in, [16, 16])
            turned_hi(0, 0, h_hi)
            square(1, lambda t: h[:, t, :], x_in, [16, 16])
            turned_hi(1, 4, y_hi)
            units(FIRST["even_a"] + 1)
            act.wait_ge(unit_used, last("mem_kv"))
            for t in range(NT):
                act.activation(mk[:, t, :], bank(2 * t), ACT.Copy).then_inc(mk_copied, 1)
            units(FIRST["even_a"] + 2)
            for t in range(NT):
                act.wait_ge(mk_copied, t + 1)
                head_square(t, mk[:, t, :].rearrange("p (a b) -> p a b", a=4), 4, P)
            units(last("even_a") + 2)
            act.wait_ge(lb_sub, 1)
            act.activation(lb[:, 0, :], lb_d[:, :], ACT.Sigmoid).then_inc(lb_sig, 1)
            for u in range(4):
                act.wait_ge(unit_used, FIRST["even_qf"] + u + 1)
                dst = (hq if u < 2 else hf)[:, 2 * (u % 2):2 * (u % 2) + 2, :].rearrange("p a b -> p (a b)")
                act.activation(dst, bank(u), ACT.Copy if u < 2 else ACT.Sigmoid).then_inc(qf_evac, 1)
                units(FIRST["even_qf"] + u + 3)
            act.wait_ge(f_done, 1)
            act.activation(whole(hf), whole(hf), ACT.Ln).then_inc(ln_done, 1)
            units(FIRST["even_ig"] + 3)
            act.wait_ge(cum_done, 1)
            act.activation(whole(he), whole(hc), ACT.Exp).then_inc(exp_done, 1)
            act.activation(whole(hd), whole(hc), ACT.Exp, scale=-1.0).then_inc(exp_done, 1)
            units(FIRST["even_ig"] + 4)
            act.wait_ge(last_done, 1)
            act.activation(whole(hf), whole(hf), ACT.Exp).then_inc(exp3_done, 1)
            units(last("even_ig") + 1)
            act.wait_ge(unit_used, last("even_ig"))
            for t in range(NT):
                act.activation(hg[:, t, :], bank(4 + 2 * t + 1), ACT.Silu).then_inc(hg_evac, 1)
            units(last("even_ig") + 2)
            for b in range(2):
                act.wait_ge(a_turned, b + 1)
                act.activation(q_t[:, :, b * P:(b + 1) * P], split4(bank(b)), ACT.Copy, scale=HD ** -0.5).then_inc(a_evac, 1)
            act.wait_ge(a_turned, 3)
            act.activation(k_t[:, :], ps[:, 2, :S], ACT.Copy).then_inc(a_evac, 1)
            for t in range(NT):
                act.wait_ge(kend_turned, t + 1)
                act.activation(kend[:, t, :], bank(6 + t), ACT.Copy).then_inc(kend_evac, 1)
            for t in range(NT):
                act.wait_ge(o_made, t + 1)
                head_square(2 + t, split4(bank(t)), 4, P)
            for t in range(NT):
                act.wait_ge(mk_turned, t + 1)
                act.activation(mk_t[:, :, t * P:(t + 1) * P], split4(bank(6 + t)), ACT.Copy).then_inc(mk_evac, 1)
            act.wait_ge(head_sum, 4)
            for hh in range(8):
                exps("a", hh)
            act.wait_ge(maxed, 9 - 1)
            act.wait_ge(dve_sink, 1)
            act.activation(esnk[:, :, :], snk[:, :, :], ACT.Exp).then_inc(act_sink, 1)
            turned_hi(2, 4, y_hi)
            units(last("even_out") + 1)
            act.wait_ge(unit_used, last("even_out"))
            square(2, lambda t: two_banks(2 * t), unit_used, [last("even_out")] * 2)
            units(last("even_out") + 2)
            square(3, lambda t: h[:, t, :], resid, [1, 2])
            turned_hi(3, 4, y_hi)
            feed_forward(0)
            square(4, lambda t: two_banks(4 + 2 * t), unit_used, [last("down0")] * 2)
            square(5, lambda t: h[:, t, :], resid, [3, 4])
            turned_hi(4, 0, y_hi)

            units(last("odd_q") + 1)
            act.wait_ge(unit_used, last("odd_q"))
            for t in range(NT):
                act.activation(q1[:, t, :], two_banks(4 + 2 * t), ACT.Copy).then_inc(q_evac, 1)
            units(last("odd_k") + 1)
            act.wait_ge(unit_used, last("odd_k"))
            act.activation(k1[:, 0, :], two_banks(0), ACT.Copy).then_inc(k_evac, 1)
            units(last("odd_v") + 1)
            for b in range(4):
                act.wait_ge(qk_turned, b + 1)
                act.activation(token_half(q1_t, b % 2, b // 2), split4(bank(b)), ACT.Copy, scale=HD ** -0.5).then_inc(qk_evac, 1)
            for b in range(2):
                act.wait_ge(qk_turned, 4 + b + 1)
                act.activation(token_half(k1_t, b % 2, b // 2), split4(bank(4 + b)), ACT.Copy).then_inc(qk_evac, 1)
            units(last("odd_v") + 2)
            for hh in range(16):
                exps("c", hh)
            turned_hi(5, 0, y_hi)
            units(last("odd_out") + 1)
            square(6, lambda t: two_banks(4 + 2 * t), unit_used, [last("odd_out")] * 2)
            units(last("odd_out") + 2)
            square(7, lambda t: h[:, t, :], resid, [5, 6])
            turned_hi(6, 0, y_hi)
            feed_forward(1)
            square(8, lambda t: two_banks(4 + 2 * t), unit_used, [last("down1")] * 2)
            square(9, lambda t: h[:, t, :], resid, [7, 8])
            turned_hi(7, 0, y_hi)

            units(last("moba_qk") + 1)
            act.wait_ge(unit_used, last("moba_qk"))
            act.activation(qkm[:, 0, :], two_banks(4), ACT.Copy).then_inc(m_evac, 1)
            units(last("moba_qk") + 2)
            act.wait_ge(m_evac, 2)
            for t in range(NT):
                head_square(4 + t, qkm[:, t, :].rearrange("p (a b) -> p a b", a=16), 16, HD)
            units(last("both_v") + 1)
            act.wait_ge(unit_used, last("both_v"))
            act.activation(v2[:, 0, :], two_banks(0), ACT.Copy).then_inc(v2_evac, 1)
            units(last("fox_qk") + 1)
            act.wait_ge(unit_used, last("fox_qk"))
            act.activation(qkf[:, 0, :], two_banks(4), ACT.Copy).then_inc(f_evac, 1)
            units(last("fox_qk") + 2)
            act.wait_ge(f_evac, 2)
            for t in range(NT):
                act.wait_ge(head_sum, 5 + t)
                head_square(6 + t, qkf[:, t, :].rearrange("p (a b) -> p a b", a=16), 16, HD)
            units(last("mem_q") + 1)
            act.wait_ge(unit_used, last("mem_q"))
            for t in range(NT):
                act.activation(qc[:, t, :], bank(2 * t + 1), ACT.Copy).then_inc(c_evac, 1)
            units(last("mem_q") + 2)
            for t in range(NT):
                act.wait_ge(head_sum, 7 + t)
                act.wait_ge(c_evac, t + 1)
                head_square(8 + t, qc[:, t, :].rearrange("p (a b) -> p a b", a=4), 4, P)
            act.wait_ge(forget, 1)
            act.activation(fz[:, 2, :, :], fz[:, 1, :, :], ACT.Exp, scale=-1.0).then_inc(forget_e, 1)
            act.wait_ge(forget_e, 1)
            act.activation(fz[:, 3, :, :], fz[:, 2, :, :], ACT.Ln, bias=1.0).then_inc(forget_l, 1)

            def gate_copy(u):
                act.wait_ge(unit_used, FIRST["gates"] + u + 1)
                act.activation(gate[:, 2 * u:2 * u + 2, :].rearrange("p a b -> p (a b)"), bank(6 + u % 2), ACT.Copy).then_inc(gate_evac, 1)

            def heads_copy(first, n, dst, q_tiles, base):
                for b in range(n):
                    kh, t = b % 2, b // 2
                    act.wait_ge(heads_turned, first + b + 1)
                    act.activation(token_half(dst, kh, t), split4(bank(base + b)), ACT.Copy,
                                   scale=HD ** -0.5 if kh == 0 else 1.0).then_inc(heads_evac, 1)

            heads_copy(0, 4, qkm_t, 4, 2)
            gate_copy(0)
            units(FIRST["gates"] + 3)
            heads_copy(4, 4, qkf_t, 4, 2)
            gate_copy(1)
            for t in range(NT):
                act.wait_ge(heads_turned, 8 + t + 1)
                act.activation(qc_t[:, :, t * P:(t + 1) * P], split4(bank(2 + t)), ACT.Copy, scale=P ** -0.5).then_inc(heads_evac, 1)
            for k in range(10):
                units(FIRST["gates"] + k + 4)
                for stage, hh in third_heads(k):
                    exps(stage, hh)
                if k >= 1:
                    gate_copy(k + 1)
            gate_copy(11)
            act.wait_ge(gate_evac, 12)
            for b in range(3):
                g = gate[:, 8 * b:8 * b + 8, :].rearrange("p a b -> p (a b)")
                act.activation(g, g, ACT.Sigmoid).then_inc(gate_sig, 1)
            for b in range(6):
                act.wait_ge(br_turned, b + 1)
                act.activation(branch_y(0, b // 2, b % 2), split4(bank(b)), ACT.Copy).then_inc(br_hi, 1)
            units(FIRST["merge_out"])
            for c in range(2):
                act.wait_ge(br_sum, 2 + c + 1)
                act.activation(h_hi[:, 4 * c:4 * c + 4, :], m_sum[:, 4 * c:4 * c + 4, :], ACT.Copy).then_inc(merged_hi, 1)
                units(FIRST["merge_out"] + c + 1)
            units(last("merge_out") + 2)
            square(10, lambda t: h[:, t, :], resid, [9, 10])
            turned_hi(8, 0, y_hi)
            feed_forward(2)
            assert done[0] == UNITS

        @block.tensor
        def _(pe):
            def wait_unit(n):
                pe.wait_ge(lo_done, n + 1)

            def tokens_by(name, base, y, splits=((0, 512), (512, 512))):
                yh, yl = y
                n0, nu, nk, cols = FIRST[name], COUNT[name], NK[name], COLS[name]
                total = sum(WIDTH[n0:n0 + nu]) // cols
                k = 0
                for n in range(n0, n0 + nu):
                    wait_unit(n)
                    for kk in range(WIDTH[n] // cols):
                        for t in range(NT):
                            tok = slice(t * P, (t + 1) * P)
                            for x, w, first, final in ((yh, hi, True, False), (yh, lo, False, False), (yl, hi, False, True)):
                                for half_, (c0, cw) in enumerate(splits):
                                    mm = pe.matmul(ps[:, base + 2 * t + half_, :cw], x[:, k, tok],
                                                   w[:, n % SPLIT, kk * cols + c0:kk * cols + c0 + cw],
                                                   start=first and k == 0, stop=final and k == total - 1)
                        k += 1
                    mm.then_inc(unit_used, 1)

            def features_of(n, s, outs, y, nk=KD, cols=256):
                pe.wait_ge(lo_done, n + 1)
                yh, yl = y
                for f, dst in enumerate(outs):
                    for k in range(nk):
                        at = slice(k * cols + f * P, k * cols + (f + 1) * P)
                        for w, x, first, final in ((hi, yh, True, False), (hi, yl, False, False), (lo, yh, False, True)):
                            mm = pe.matmul(dst, w[:, s % SPLIT, at], x(k), start=first and k == 0, stop=final and k == nk - 1)
                mm.then_inc(unit_used, 1)

            def of_tiles(y):
                return tuple((lambda k, part=part: part[:, k, :]) for part in y)

            def turn(stage, src, base, ready, count):
                for t in range(NT):
                    pe.wait_ge(ready, count[t])
                    for kh in range(2):
                        for kk in range(4):
                            mm = pe.transpose(ps[:, base + 2 * t + kh, kk * P:(kk + 1) * P],
                                              src[:, t, (4 * kh + kk) * P:(4 * kh + kk + 1) * P], ident[:, :])
                        mm.then_inc(turned, 1)

            def turn_heads(src, t, c0, b, signal, n=4):
                for kk in range(n):
                    mm = pe.transpose(ps[:, b, kk * P:(kk + 1) * P], src[:, t, c0 + kk * P:c0 + (kk + 1) * P], ident[:, :])
                mm.then_inc(signal, 1)

            def operands(stage, hh):
                if stage == "a":
                    g, p = hh // 4, hh % 4
                    r = slice(64 * g, 64 * g + 64)
                    return q_t[r, p, :], k_t[r, :], lambda kt: va[:, kt, 64 * g:64 * g + 64]
                if stage == "x":
                    return qc_t[:, hh, :], mk_t[:, hh, :], lambda kt: mv[:, kt, hh * P:(hh + 1) * P]
                r = slice(64 * (hh % 2), 64 * (hh % 2) + 64)
                if stage == "c":
                    return q1_t[r, hh // 2, :], k1_t[r, hh // 2, :], lambda kt: v1[:, kt, hh * HD:(hh + 1) * HD]
                tile = qkm_t if stage == "m" else qkf_t
                off = 0 if stage == "m" else 512
                return tile[r, hh // 2, :], tile[r, 4 + hh // 2, :], lambda kt: v2[:, kt, off + hh * HD:off + (hh + 1) * HD]

            def place(stage, hh, t):
                if stage == "c":
                    return ps[:, 4 + 2 * t + hh // 8, (hh % 8) * HD:(hh % 8 + 1) * HD]
                d = ATT[stage][2]
                return ps[:, 4 + t, hh * d:(hh + 1) * d]

            def scores(stage, hh):
                a = ATT[stage][0] + hh
                q, k, _ = operands(stage, hh)
                if a >= 2:
                    pe.wait_ge(powed, a - 1)
                for t in range(NT):
                    n = S if stage == "x" else P * (t + 1)
                    c0 = S * t if stage == "x" else P * t
                    dst = ps[:, a % 2, c0:c0 + n]
                    mm = pe.matmul(dst, q[:, t * P:(t + 1) * P], k[:, :n], start=True, stop=stage != "f")
                    if stage == "f":
                        r = slice(64 * (hh % 2), 64 * (hh % 2) + 64)
                        mm = pe.matmul(dst, pick[r, hh, :], ncum[r, :n], start=False, stop=True)
                mm.then_inc(scored, 1)

            def turn_probs(stage, hh):
                a = ATT[stage][0] + hh
                pe.wait_ge(powed, a + 1)
                if a >= 2:
                    pe.wait_ge(probs_copied, a - 1)
                for i in range(4 if stage == "x" else 3):
                    mm = pe.transpose(ps[:, 2 + a % 2, i * P:(i + 1) * P], pr[:, a % 2, i * P:(i + 1) * P], ident[:, :])
                mm.then_inc(probs_turned, 1)

            def mix(stage, hh):
                a = ATT[stage][0] + hh
                _, _, v = operands(stage, hh)
                pe.wait_ge(probs_copied, a + 1)
                i = 0
                for t in range(NT):
                    kts = range(2 if stage == "x" else t + 1)
                    for kt in kts:
                        mm = pe.matmul(place(stage, hh, t), pt[:, a % 2, i * P:(i + 1) * P], v(kt),
                                       start=kt == 0, stop=kt == kts[-1])
                        i += 1
                mm.then_inc(mixed, 1)

            def attention(stage, n):
                for i in range(n + 2):
                    if i < n:
                        scores(stage, i)
                    if 1 <= i <= n:
                        turn_probs(stage, i - 1)
                    if i >= 2:
                        mix(stage, i - 2)

            Y = (y_hi, y_lo)
            pe.wait_ge(ident_in, 16)
            turn(0, xhat, 0, normed, [1, 2])
            turn(1, xhat, 4, normed, [3, 4])
            pe.wait_ge(y_lo_done, 4)
            tokens_by("mem_kv", 0, (h_hi, h_lo))
            pe.wait_ge(y_lo_done, 8)
            tokens_by("even_a", 4, Y, ((0, 512), (512, 256)))
            pe.wait_ge(mk_copied, 2)
            pe.wait_ge(mv_copied, 2)
            for u in range(4):
                n = FIRST["even_qf"] + u
                features_of(n, n % RAW, [ps[:, u, f * S:(f + 1) * S] for f in range(2)], of_tiles(Y))
            pe.wait_ge(roped, 2)
            tokens_by("even_ig", 4, Y)
            pe.wait_ge(qf_evac, 4)
            for t in range(NT):
                for p in range(4):
                    mm = pe.transpose(ps[:, t, p * P:(p + 1) * P],
                                      qk[:, t, p * P:(p + 1) * P], ident[:, :])
                mm.then_inc(a_turned, 1)
            for t in range(NT):
                mm = pe.transpose(ps[:, 2, t * P:(t + 1) * P], qk[:, t, 512:640], ident[:, :])
            mm.then_inc(a_turned, 1)
            pe.wait_ge(hg_evac, 2)
            pe.wait_ge(hv_evac, 2)
            pe.wait_ge(dec_done, 3)
            for t in range(NT):
                for hh in range(HB):
                    mm = pe.transpose(ps[:, 6 + t, hh * P:(hh + 1) * P], hc[:, hh, t * P:(t + 1) * P], ident[:, :])
                mm.then_inc(kend_turned, 1)
            for t in range(NT):
                tok = slice(t * P, (t + 1) * P)
                for hh in range(HB):
                    mm = pe.matmul(ps[:, 3 + t, hh * P:(hh + 1) * P], hd[:, hh, tok], hq[:, hh, tok], start=True, stop=True)
                mm.then_inc(st_made, 1)
            pe.wait_ge(kend_evac, 2)
            for b in range(NBLK - 1):
                if b >= 3:
                    pe.wait_ge(stated, b - 2)
                r = slice(BLK * (b % 4), BLK * (b % 4) + BLK)
                for hh in range(HB):
                    mm = pe.matmul(ps[:, 5 + b % 3, hh * P:(hh + 1) * P], kend[r, b // 4, hh * P:(hh + 1) * P],
                                   hv[r, b // 4, hh * P:(hh + 1) * P], start=True, stop=True)
                mm.then_inc(kv_made, 1)
            pe.wait_ge(a_evac, 3)
            for t in range(NT):
                pe.wait_ge(st_evac, t + 1)
                pe.wait_ge(stated, 3 + 4 * t)
                for hh in range(HB):
                    cols = slice(hh * P, (hh + 1) * P)
                    mm = pe.matmul(ps[:, t, cols], s_t[:, t, hh, :], hv[:, t, cols], start=True, stop=True, skip_group_check=True)
                    for b in range(max(4 * t, 1), 4 * t + 4):
                        j = b % 4
                        mm = pe.matmul(ps[BLK * j:BLK * j + BLK, t, cols], hq[:, hh, b * BLK:(b + 1) * BLK],
                                       state[b - 1][:, hh, :], start=False, stop=True, skip_group_check=True)
                mm.then_inc(o_made, 1)
            pe.wait_ge(mk_ready, 2)
            pe.wait_ge(stated, 7)
            for t in range(NT):
                turn_heads(mk, t, 0, 6 + t, mk_turned)
            pe.wait_ge(hgrn_out, 2)
            attention("a", 8)
            pe.wait_ge(mk_evac, 2)
            turn(2, xhat, 4, attended, [2, 2])
            pe.wait_ge(y_lo_done, 12)
            tokens_by("even_out", 0, Y)

            def feed_forward(layer, base):
                up = FIRST[f"up{layer}"]
                for j in range(KF):
                    if j >= 4:
                        pe.wait_ge(hmul, KF * layer + j - 3)
                    features_of(up + j, (up + j) % RAW, [ps[:, j % 4, f * S:(f + 1) * S] for f in range(2)], of_tiles(Y))
                n0 = FIRST[f"down{layer}"]
                for u in range(KF // 2):
                    wait_unit(n0 + u)
                    pe.wait_ge(h_lo_done, KF * layer + 2 * u + 2)
                    for kk in range(2):
                        k = 2 * u + kk
                        for t in range(NT):
                            tok = slice(t * P, (t + 1) * P)
                            for x, w, first, final in ((h_hi, hi, True, False), (h_hi, lo, False, False), (h_lo, hi, False, True)):
                                for c in range(2):
                                    mm = pe.matmul(ps[:, base + 2 * t + c, :], x[:, k, tok],
                                                   w[:, (n0 + u) % SPLIT, kk * D + c * 512:kk * D + (c + 1) * 512],
                                                   start=first and k == 0, stop=final and k == KF - 1)
                    mm.then_inc(unit_used, 1)

            turn(3, xhat, 4, normed, [5, 6])
            pe.wait_ge(y_lo_done, 16)
            feed_forward(0, 4)
            turn(4, xhat, 0, normed, [7, 8])
            pe.wait_ge(y_lo_done, 20)
            tokens_by("odd_q", 4, Y)
            tokens_by("odd_k", 0, Y)
            pe.wait_ge(q_evac, 2)
            tokens_by("odd_v", 4, Y)
            pe.wait_ge(k_evac, 2)
            for b in range(4):
                turn_heads(q1, b // 2, 512 * (b % 2), b, qk_turned)
            pe.wait_ge(v_evac, 2)
            for b in range(4):
                turn_heads(k1, b // 2, 512 * (b % 2), 4 + b, qk_turned)
            pe.wait_ge(qk_evac, 6)
            pe.wait_ge(k_copied, 2)
            attention("c", 16)
            turn(5, xhat, 0, attended, [3, 4])
            pe.wait_ge(y_lo_done, 24)
            tokens_by("odd_out", 4, Y)
            turn(6, xhat, 0, normed, [9, 10])
            pe.wait_ge(y_lo_done, 28)
            feed_forward(1, 4)
            turn(7, xhat, 0, normed, [11, 12])
            pe.wait_ge(y_lo_done, 32)
            tokens_by("moba_qk", 4, Y)
            tokens_by("both_v", 0, Y)
            pe.wait_ge(m_evac, 2)
            tokens_by("fox_qk", 4, Y)
            pe.wait_ge(v2_evac, 2)
            tokens_by("mem_q", 0, Y, ((0, 8), (8, 512)))

            def gate_unit(u):
                n = FIRST["gates"] + u
                if u >= 2:
                    pe.wait_ge(gate_evac, u - 1)
                features_of(n, n % RAW, [ps[:, 6 + u % 2, f * S:(f + 1) * S] for f in range(2)], of_tiles(Y))

            pe.wait_ge(c_evac, 2)
            pe.wait_ge(z_done, 2)
            pe.wait_ge(f_evac, 2)
            for b in range(4):
                pe.wait_ge(m_ready, b // 2 + 1)
                turn_heads(qkm, b // 2, 512 * (b % 2), 2 + b, heads_turned)
            gate_unit(0)
            pe.wait_ge(heads_evac, 4)
            for b in range(4):
                pe.wait_ge(f_ready, b // 2 + 1)
                turn_heads(qkf, b // 2, 512 * (b % 2), 2 + b, heads_turned)
            gate_unit(1)
            pe.wait_ge(heads_evac, 8)
            for t in range(NT):
                pe.wait_ge(c_ready, t + 1)
                turn_heads(qc, t, 0, 2 + t, heads_turned)
            pe.wait_ge(nlf_ready, 1)
            for t in range(NT):
                mm = pe.transpose(ps[:, 4, t * P:(t + 1) * P], nlf[:, t, :], ident[:, :])
            mm.then_inc(heads_turned, 1)
            pe.wait_ge(heads_evac, 10)
            pe.wait_ge(ncum_done, 1)
            for k in range(10):
                now, before = third_heads(k), third_heads(k - 1) if k else []
                for stage, hh in now:
                    scores(stage, hh)
                for stage, hh in before:
                    if hh == 0 and stage != "m":
                        pe.wait_ge(attended, ATTENDED[stage])
                    mix(stage, hh)
                gate_unit(k + 2)
                for stage, hh in now:
                    turn_probs(stage, hh)
            for stage, hh in third_heads(9):
                mix(stage, hh)
            pe.wait_ge(gate_evac, 12)
            for b in range(6):
                pe.wait_ge(attended, 4 + b + 1)
                turn_heads((qkm, qkf, qkm)[b // 2], b % 2, 512 * (b // 4), b, br_turned)
            for u in range(6):
                n = FIRST["branches"] + u
                b = u // 2
                pe.wait_ge(br_lo, 6 if u == 0 else 1)
                if u >= 2:
                    pe.wait_ge(br_used, u - 1)
                if b == 2:
                    ys = tuple((lambda k, part=part: part[:, 16 + k, :]) for part in (h_hi, h_lo))
                else:
                    ys = tuple((lambda k, part=part: part[:, 4 * b + k, :]) for part in Y)
                outs = [ps[:, 2 * (u % 2) + f // 2, (f % 2) * S:(f % 2 + 1) * S] for f in range(4)]
                features_of(n, n % RAW, outs, ys, 4, 512)
            pe.wait_ge(merged_lo, 2)
            tokens_by("merge_out", 4, (h_hi, h_lo))
            turn(8, xhat, 0, normed, [13, 14])
            pe.wait_ge(y_lo_done, 36)
            feed_forward(2, 4)

        @block.vector
        def _(dve):
            done, links = [0], [0]

            def split_unit(n, s=None, w=None):
                s = n % RAW if s is None else s
                w = WIDTH[n] if w is None else w
                dve.wait_ge(hi_done, n + 1)
                dve.tensor_tensor(lo[:, s % SPLIT, :w], raw[:, s, :w], hi[:, s % SPLIT, :w].bitcast(F32), ALU.subtract).then_inc(lo_done, 1)

            def units(upto):
                while done[0] < upto:
                    split_unit(done[0])
                    done[0] += 1

            def link(ins):
                links[0] += 1
                ins.then_inc(dve_link, 1)
                dve.wait_ge(dve_link, links[0])

            def gain_wait(g):
                dve.wait_ge(gain_in[g % 2], 16 * (g // 2 + 1))

            def norm(g, r, src):
                gain_wait(g)
                if r >= 2:
                    dve.wait_ge(turned, 4 * (TURN_OF_NORM[r] - 1) + 4)
                for t in range(NT):
                    dve.wait_ge(rooted, 2 * g + t + 1)
                    if r == 1:
                        dve.wait_ge(turned, 2 * t + 2)
                    dve.scalar_tensor_tensor(xhat[:, t, :], src[:, t, :], rstd[:, g % 2, t:t + 1], gain[:, g % 2, :],
                                             ALU.mult, ALU.mult).then_inc(normed, 1)

            def turned_lo(stage, base, dst, dst_hi):
                for t in range(NT):
                    for kh in range(2):
                        dve.wait_ge(y_hi_done, 4 * stage + 2 * t + kh + 1)
                        dve.tensor_tensor(token_half(dst, kh, t), split4(bank(base + 2 * t + kh)),
                                          token_half(dst_hi, kh, t).bitcast(F32), ALU.subtract).then_inc(y_lo_done, 1)

            def post_norm(g, p, base):
                gain_wait(g)
                for t in range(NT):
                    dve.wait_ge(rooted, 2 * g + t + 1)
                    dve.scalar_tensor_tensor(xhat[:, t, :], two_banks(base + 2 * t), rstd[:, g % 2, t:t + 1], gain[:, g % 2, :],
                                             ALU.mult, ALU.mult).then_inc(post_mul, 1)
                    dve.wait_ge(post_mul, 2 * p + t + 1)
                    dve.tensor_tensor(h[:, t, :], h[:, t, :], xhat[:, t, :], ALU.add).then_inc(resid, 1)

            def add_residual(name, base):
                dve.wait_ge(unit_used, last(name))
                for t in range(NT):
                    dve.tensor_tensor(h[:, t, :], two_banks(base + 2 * t), h[:, t, :], ALU.add).then_inc(resid, 1)

            def head_sums(i, nh, d):
                dve.wait_ge(head_sq, i + 1)
                dve.tensor_reduce(hs[:, i % 2, :nh], whole(junk[i % 2])[:, :nh * d].rearrange("p (a b) -> p a b", a=nh),
                                  AX.X, ALU.add).then_inc(head_sum, 1)

            def head_scale(i, out_, src, nh, d):
                dve.wait_ge(head_root, i + 1)
                link(dve.tensor_tensor(out_, src, hr[:, i % 2, :nh].rearrange("p (a b) -> p a b", b=1).to_broadcast([P, nh, d]), ALU.mult))

            def head_gains(out_, nh, d, off):
                g = head_gain[:, off:off + d].rearrange("p (a b) -> p a b", a=1).to_broadcast([P, nh, d])
                return dve.tensor_tensor(out_, out_, g, ALU.mult)

            def heads_view(ap, d):
                return ap.rearrange("p (a b) -> p a b", b=d)

            def scores_max(stage, hh):
                a, col = ATT[stage][0] + hh, COLUMN[stage] + hh
                dve.wait_ge(scored, a + 1)
                if a >= 2:
                    dve.wait_ge(powed, a - 1)
                if stage == "x":
                    dve.tensor_reduce(top[:, col, :], ps[:, a % 2, :].rearrange("p (t k) -> p t k", t=NT), AX.X, ALU.max).then_inc(row_max, 1)
                else:
                    if stage == "c":
                        dve.wait_ge(bias_in[hh % 2], 32 * (hh // 2 + 1))
                    for t in range(NT):
                        c = slice(P * t, P + S * t)
                        add = {"a": window[:, c], "m": causal[:, c], "f": causal[:, c]}.get(stage)
                        if stage == "c":
                            add = bias[:, hh % 2, (P if t == 0 else 0):S]
                        init = rows_in[:, hh:hh + 1] if stage == "a" else MASKED
                        ins = dve.tensor_tensor_reduce(sc[:, a % 2, c], ps[:, a % 2, c], add, 1.0, init, ALU.add, ALU.max,
                                                       top[:, col, t:t + 1])
                    ins.then_inc(row_max, 1)
                dve.wait_ge(row_max, a + 1)
                dve.tensor_scalar(neg[:, col, :], top[:, col, :], -1.0, None, ALU.mult).then_inc(maxed, 1)

            def probs_copy(stage, hh):
                a = ATT[stage][0] + hh
                n = 512 if stage == "x" else 384
                dve.wait_ge(probs_turned, a + 1)
                if a >= 2:
                    dve.wait_ge(mixed, a - 1)
                dve.tensor_copy(pt[:, a % 2, :n], ps[:, 2 + a % 2, :n]).then_inc(probs_copied, 1)

            def attention(stage, n):
                for i in range(n + 1):
                    if i < n:
                        scores_max(stage, i)
                    if i >= 1:
                        probs_copy(stage, i - 1)

            def scale_outputs(stage, dst):
                a, n, d = ATT[stage]
                dve.wait_ge(mixed, a + n)
                cols = slice(COLUMN[stage], COLUMN[stage] + n)
                link(dve.reciprocal(rec[:, cols, :], tot[:, cols, :]))
                for t in range(NT):
                    src = two_banks(4 + 2 * t) if stage == "c" else bank(4 + t)
                    dve.tensor_tensor(dst(t).rearrange("p (a b) -> p a b", b=d), src.rearrange("p (a b) -> p a b", b=d),
                                      rec[:, cols, t:t + 1].to_broadcast([P, n, d]), ALU.mult).then_inc(attended, 1)

            TURN_OF_NORM = {0: 0, 1: 1, 2: 3, 3: 4, 4: 6, 5: 7, 6: 8}

            def feed_forward(layer):
                up = FIRST[f"up{layer}"]
                J0 = KF * layer

                def low(j):
                    dve.wait_ge(h_hi_done, J0 + j + 1)
                    dve.tensor_tensor(h_lo[:, j, :], pt[:, j % 2, :S], h_hi[:, j, :].bitcast(F32), ALU.subtract).then_inc(h_lo_done, 1)

                for j in range(KF):
                    if layer < 2:
                        c = sc[:, j % 2, :S]
                        dve.wait_ge(conv_begun, J0 + j + 1)
                        link(dve.scalar_tensor_tensor(c[:, 1:S], ps[:, j % 4, 0:S - 1], conv[:, layer, j, 1:2], c[:, 1:S], ALU.mult, ALU.add))
                        dve.scalar_tensor_tensor(c[:, 2:S], ps[:, j % 4, 0:S - 2], conv[:, layer, j, 0:1], c[:, 2:S],
                                                 ALU.mult, ALU.add).then_inc(conv_done, 1)
                    if j >= 1:
                        low(j - 1)
                    units(up + j + 3)
                    dve.wait_ge(glued, J0 + j + 1)
                    dve.tensor_tensor(pt[:, j % 2, :S], ps[:, j % 4, S:2 * S], pr[:, j % 2, :S], ALU.mult).then_inc(hmul, 1)
                low(KF - 1)
                units(last(f"down{layer}") + (2 if layer < 2 else 0))

            units(2)
            norm(0, 0, mem_x)
            turned_lo(0, 0, h_lo, h_hi)
            dve.wait_ge(x_in, 16)
            norm(1, 1, h)
            turned_lo(1, 4, y_lo, y_hi)
            units(FIRST["even_a"] + 1)
            dve.wait_ge(unit_used, last("mem_kv"))
            for t in range(NT):
                dve.tensor_copy(mv[:, t, :], bank(2 * t + 1)).then_inc(mv_copied, 1)
            units(FIRST["even_a"] + 2)
            dve.wait_ge(const_in, 16 * 12)
            dve.wait_ge(set_up, 4)
            for t in range(NT):
                head_sums(t, 4, P)
            for t in range(NT):
                v = heads_view(mk[:, t, :], P)
                head_scale(t, v, v, 4, P)
                head_gains(v, 4, P, 384).then_inc(mk_ready, 1)
                units(FIRST["even_a"] + 3 + t)
            dve.tensor_tensor(lb_d[:, :], lb_in[:, 0, :], lb_in[:, 1, :], ALU.subtract).then_inc(lb_sub, 1)
            dve.wait_ge(lb_sig, 1)
            dve.tensor_scalar(lb[:, 1, :], lb[:, 0, :], -1.0, 1.0, ALU.mult, ALU.add).then_inc(lb_done, 1)
            units(last("even_a") + 1)
            dve.wait_ge(unit_used, last("even_a"))
            for t in range(NT):
                x = heads_view(two_banks(4 + 2 * t)[:, :640], HD)
                o = heads_view(qk[:, t, :], HD)
                w = heads_view(rot[:, :], HD)
                cos, sin, nsin = (rope_a[:, i, t:t + 1, :].to_broadcast([P, 10, 32]) for i in range(3))
                dve.tensor_tensor(o[:, :, 0:32], x[:, :, 0:32], cos, ALU.mult)
                dve.tensor_tensor(o[:, :, 32:64], x[:, :, 32:64], cos, ALU.mult)
                dve.tensor_tensor(w[:, :, 0:32], x[:, :, 32:64], nsin, ALU.mult)
                dve.tensor_copy(va[:, t, :], two_banks(4 + 2 * t)[:, 640:768])
                link(dve.tensor_tensor(w[:, :, 32:64], x[:, :, 0:32], sin, ALU.mult))
                dve.tensor_tensor(qk[:, t, :], qk[:, t, :], rot[:, :], ALU.add).then_inc(roped, 1)
                dve.wait_ge(roped, t + 1)
                units(last("even_a") + 2 + t)
            units(last("even_qf") + 1)
            dve.wait_ge(qf_evac, 4)
            dve.wait_ge(lb_done, 1)
            for hh in range(HB):
                ins = dve.tensor_scalar(hf[:, hh, :], hf[:, hh, :], lb[:, 1, hh:hh + 1], lb[:, 0, hh:hh + 1], ALU.mult, ALU.add)
            link(ins)
            dve.tensor_scalar(whole(hk), whole(hf), -1.0, 1.0, ALU.mult, ALU.add).then_inc(f_done, 1)
            units(FIRST["even_ig"] + 2)
            dve.wait_ge(ln_done, 1)
            for hh in range(HB):
                ins = dve.tensor_tensor_scan(hc[:, hh, :], keep[:, :], hf[:, hh, :], 0.0, ALU.mult, ALU.add)
            ins.then_inc(cum_done, 1)
            dve.wait_ge(cum_done, 1)
            blocks = whole(hc).rearrange("p (n l) -> p n l", l=BLK)
            dve.tensor_tensor(whole(hf).rearrange("p (n l) -> p n l", l=BLK), blocks[:, :, BLK - 1:BLK].to_broadcast([P, HB * NBLK, BLK]),
                              blocks, ALU.subtract).then_inc(last_done, 1)
            units(FIRST["even_ig"] + 3)
            dve.wait_ge(exp_done, 2)
            dve.tensor_tensor(whole(hq), whole(hq), whole(he), ALU.mult).then_inc(dec_done, 1)
            dve.tensor_tensor(whole(hd), whole(hk), whole(hd), ALU.mult).then_inc(dec_done, 1)
            units(FIRST["even_ig"] + 4)
            dve.wait_ge(exp3_done, 1)
            dve.tensor_tensor(whole(hc), whole(hk), whole(hf), ALU.mult).then_inc(dec_done, 1)
            units(last("even_ig") + 1)
            dve.wait_ge(unit_used, last("even_ig"))
            for t in range(NT):
                dve.tensor_copy(hv[:, t, :], bank(4 + 2 * t)).then_inc(hv_evac, 1)
            units(last("even_ig") + 2)
            mask = block_causal[:, :].rearrange("p (a b) -> p a b", a=1).to_broadcast([P, HB, P])
            for t in range(NT):
                dve.wait_ge(st_made, t + 1)
                dve.copy_predicated(s_t[:, t, :, :], mask, split4(bank(3 + t))).then_inc(st_evac, 1)
            decay = whole(he).rearrange("p (h n l) -> p h n l", h=HB, l=BLK)
            dve.wait_ge(dec_done, 3)
            for b in range(NBLK - 1):
                dve.wait_ge(kv_made, b + 1)
                kv = split4(bank(5 + b % 3))
                if b == 0:
                    dve.tensor_copy(state[0], kv).then_inc(stated, 1)
                    continue
                dve.wait_ge(stated, b)
                for hh in range(HB):
                    ins = dve.scalar_tensor_tensor(state[b][:, hh, :], state[b - 1][:, hh, :], decay[:, hh, b, BLK - 1:BLK],
                                                   kv[:, hh, :], ALU.mult, ALU.add)
                ins.then_inc(stated, 1)
            dve.wait_ge(gated, 2)
            for t in range(NT):
                head_sums(2 + t, 4, P)
            for t in range(NT):
                o = heads_view(xhat[:, t, 512:1024], P)
                head_scale(2 + t, o, split4(bank(t)), 4, P)
                dve.tensor_tensor(xhat[:, t, 512:1024], xhat[:, t, 512:1024], hg[:, t, :], ALU.mult).then_inc(hgrn_out, 1)
            dve.wait_ge(hgrn_out, 2)
            attention("a", 8)
            dve.wait_ge(maxed, 8)
            dve.tensor_tensor(snk[:, :, :], neg[:, 0:8, :], rows_in[:, 0:8].rearrange("p (a b) -> p a b", b=1).to_broadcast([P, 8, 2]),
                              ALU.add).then_inc(dve_sink, 1)
            dve.wait_ge(act_sink, 1)
            link(dve.tensor_tensor(tot[:, 0:8, :], tot[:, 0:8, :], esnk[:, :, :], ALU.add))
            scale_outputs("a", lambda t: xhat[:, t, 0:512])
            turned_lo(2, 4, y_lo, y_hi)
            units(last("even_out") + 1)
            dve.wait_ge(turned, 12)
            post_norm(2, 0, 0)
            units(last("even_out") + 2)
            norm(3, 2, h)
            turned_lo(3, 4, y_lo, y_hi)
            feed_forward(0)
            dve.wait_ge(turned, 16)
            post_norm(4, 1, 4)
            norm(5, 3, h)
            turned_lo(4, 0, y_lo, y_hi)

            units(last("odd_k") + 1)
            dve.wait_ge(unit_used, last("odd_k"))
            dve.tensor_copy(k1[:, 1, :], two_banks(2)).then_inc(k_evac, 1)
            units(last("odd_v") + 1)
            dve.wait_ge(unit_used, last("odd_v"))
            for t in range(NT):
                dve.tensor_copy(v1[:, t, :], two_banks(4 + 2 * t)).then_inc(v_evac, 1)
            for b in range(2, 4):
                dve.wait_ge(qk_turned, 4 + b + 1)
                dve.tensor_copy(token_half(k1_t, b % 2, b // 2), split4(bank(4 + b))).then_inc(k_copied, 1)
            units(last("odd_v") + 2)
            dve.wait_ge(set_up, 6)
            attention("c", 16)
            dve.wait_ge(turned, 20)
            scale_outputs("c", lambda t: xhat[:, t, :])
            turned_lo(5, 0, y_lo, y_hi)
            units(last("odd_out") + 1)
            dve.wait_ge(turned, 24)
            post_norm(6, 2, 4)
            units(last("odd_out") + 2)
            norm(7, 4, h)
            turned_lo(6, 0, y_lo, y_hi)
            feed_forward(1)
            dve.wait_ge(turned, 28)
            post_norm(8, 3, 4)
            norm(9, 5, h)
            turned_lo(7, 0, y_lo, y_hi)

            units(last("moba_qk") + 1)
            dve.wait_ge(unit_used, last("moba_qk"))
            dve.tensor_copy(qkm[:, 1, :], two_banks(6)).then_inc(m_evac, 1)
            units(last("moba_qk") + 2)
            n = last("moba_qk") + 2
            for t in range(NT):
                head_sums(4 + t, 16, HD)
            for t in range(NT):
                v = heads_view(qkm[:, t, :], HD)
                head_scale(4 + t, v, v, 16, HD)
                head_gains(v[:, 0:8], 8, HD, 0)
                link(head_gains(v[:, 8:16], 8, HD, 64))
                n += 1
                units(min(n, last("both_v") + 1))
                w = [heads_view(pt[:, 0, 128 * i:128 * i + 128], 8) for i in range(4)]
                cos, sin, nsin = (rope_m[:, i, t:t + 1, :].to_broadcast([P, 16, 8]) for i in range(3))
                x1, x2 = v[:, :, 0:8], v[:, :, 8:16]
                dve.tensor_tensor(w[0], x1, cos, ALU.mult)
                dve.tensor_tensor(w[1], x2, nsin, ALU.mult)
                dve.tensor_tensor(w[2], x2, cos, ALU.mult)
                link(dve.tensor_tensor(w[3], x1, sin, ALU.mult))
                dve.tensor_tensor(x1, w[0], w[1], ALU.add)
                dve.tensor_tensor(x2, w[2], w[3], ALU.add).then_inc(m_ready, 1)
                dve.wait_ge(m_ready, t + 1)
            units(last("both_v") + 1)
            dve.wait_ge(unit_used, last("both_v"))
            dve.tensor_copy(v2[:, 1, :], two_banks(2)).then_inc(v2_evac, 1)
            units(last("fox_qk") + 1)
            dve.wait_ge(unit_used, last("fox_qk"))
            dve.tensor_copy(qkf[:, 1, :], two_banks(6)).then_inc(f_evac, 1)
            units(last("fox_qk") + 2)
            for t in range(NT):
                head_sums(6 + t, 16, HD)
            for t in range(NT):
                v = heads_view(qkf[:, t, :], HD)
                head_scale(6 + t, v, v, 16, HD)
                head_gains(v[:, 0:8], 8, HD, 128)
                head_gains(v[:, 8:16], 8, HD, 192).then_inc(f_ready, 1)
                units(min(last("fox_qk") + 3 + t, last("mem_q") + 1))
            units(last("mem_q") + 1)
            dve.wait_ge(unit_used, last("mem_q"))
            for t in range(NT):
                dve.tensor_tensor(fz[:, 0, t, :], ps[:, 2 * t, 0:8], rows_in[:, 8:16], ALU.add).then_inc(z_done, 1)
            dve.wait_ge(z_done, 2)
            dve.scalar_tensor_tensor(fz[:, 1, :, :], fz[:, 0, :, :], -1.0, fz[:, 0, :, :], ALU.mult, ALU.max).then_inc(forget, 1)
            link(dve.tensor_scalar(fz[:, 4, :, :], fz[:, 0, :, :], -1.0, 0.0, ALU.mult, ALU.max))
            units(last("mem_q") + 2)
            for t in range(NT):
                head_sums(8 + t, 4, P)
            for t in range(NT):
                v = heads_view(qc[:, t, :], P)
                head_scale(8 + t, v, v, 4, P)
                head_gains(v, 4, P, 256).then_inc(c_ready, 1)
            dve.wait_ge(forget_l, 1)
            for c in (0, 64):
                ins = dve.tensor_tensor(nlf[:, :, c:c + 8], fz[:, 4, :, :], fz[:, 3, :, :], ALU.add)
            ins.then_inc(nlf_ready, 1)
            units(FIRST["gates"] + 3)
            dve.wait_ge(heads_turned, 11)
            dve.tensor_tensor_scan(ncum[:, :], ones[:, :], ps[:, 4, :S], 0.0, ALU.mult, ALU.add).then_inc(ncum_done, 1)
            for k in range(10):
                now = third_heads(k)
                for stage, hh in now:
                    scores_max(stage, hh)
                if k == 4:
                    scale_outputs("m", lambda t: qkm[:, t, 0:512])
                if k == 8:
                    scale_outputs("f", lambda t: qkf[:, t, 0:512])
                units(FIRST["gates"] + k + 4)
                for stage, hh in now:
                    probs_copy(stage, hh)
            scale_outputs("x", lambda t: qkm[:, t, 512:1024])
            for b in range(6):
                dve.wait_ge(br_hi, b + 1)
                dve.tensor_tensor(branch_y(1, b // 2, b % 2), split4(bank(b)), branch_y(0, b // 2, b % 2).bitcast(F32),
                                  ALU.subtract).then_inc(br_lo, 1)
            for u in range(6):
                b, c = u // 2, u % 2
                units(FIRST["branches"] + u + 2)
                dve.wait_ge(unit_used, FIRST["branches"] + u + 1)
                dve.wait_ge(gate_sig, b + 1)
                src = two_banks(2 * c)
                g = gate[:, 8 * b + 4 * c:8 * b + 4 * c + 4, :].rearrange("p a b -> p (a b)")
                m = m_sum[:, 4 * c:4 * c + 4, :].rearrange("p a b -> p (a b)")
                if b == 0:
                    dve.tensor_tensor(m, src, g, ALU.mult).then_inc(br_used, 1)
                else:
                    dve.tensor_tensor(g, src, g, ALU.mult).then_inc(br_used, 1)
                    dve.wait_ge(br_used, u + 1)
                    dve.tensor_tensor(m, m, g, ALU.add).then_inc(br_sum, 1)
            for c in range(2):
                dve.wait_ge(merged_hi, c + 1)
                dve.tensor_tensor(h_lo[:, 4 * c:4 * c + 4, :], m_sum[:, 4 * c:4 * c + 4, :], h_hi[:, 4 * c:4 * c + 4, :].bitcast(F32),
                                  ALU.subtract).then_inc(merged_lo, 1)
            units(last("merge_out") + 1)
            add_residual("merge_out", 4)
            units(last("merge_out") + 2)
            norm(10, 6, h)
            turned_lo(8, 0, y_lo, y_hi)
            feed_forward(2)
            add_residual("down2", 4)
            assert done[0] == UNITS


_OUT = (1, S, D)


def kernel(**inputs):
    import concourse.bacc as bacc
    from concourse.bass_utils import run_bass_kernel_spmd

    nc = bacc.Bacc("TRN2", target_bir_lowering=False, num_devices=1)
    arrays = {**lay_out({k: np.asarray(v) for k, v in inputs.items()}), **constants()}
    arrays = {k: np.ascontiguousarray(v) for k, v in arrays.items()}
    dram = {k: nc.dram_tensor(f"in_{k}", v.shape, mybir.dt.from_np(v.dtype), kind="ExternalInput").ap() for k, v in arrays.items()}
    out = nc.dram_tensor("out", (S, D), F32, kind="ExternalOutput").ap()
    build(nc, dram, out)
    got = run_bass_kernel_spmd(nc, [{f"in_{k}": v for k, v in arrays.items()}], core_ids=[0])
    return got.results[0]["out"].reshape(_OUT)
```

```python
from contextlib import ExitStack

import numpy as np

import concourse.bass as bass
from concourse import mybir

F32 = mybir.dt.float32
F32R = mybir.dt.float32r
U32 = mybir.dt.uint32
ALU = mybir.AluOpType
ACT = mybir.ActivationFunctionType
AX = mybir.AxisListType

P = 128
S = 256
NT = S // P
D = 1024
KD = D // P
FF = 2816
KF = FF // P
HD = 64
EPS = 1e-6
MASKED = -3.0e38
CHUNK = 64
BLK = 32
NBLK = S // BLK
HB = 4
REL = 128

UNIT = 2048
RAW = 4

STREAM = [
    ("mem_kv", 4, 2, 1024),
    ("even_a", 4, 2, 768), ("even_qf", 4, 8, 256), ("even_ig", 4, 2, 1024), ("even_out", 4, 2, 1024),
    ("up0", 22, 8, 256), ("down0", 11, 2, 1024),
    ("odd_q", 4, 2, 1024), ("odd_k", 4, 2, 1024), ("odd_v", 4, 2, 1024), ("odd_out", 4, 2, 1024),
    ("up1", 22, 8, 256), ("down1", 11, 2, 1024),
    ("moba_qk", 4, 2, 1024), ("both_v", 4, 2, 1024), ("fox_qk", 4, 2, 1024), ("mem_q", 3, 3, 520),
    ("gates", 12, 8, 256), ("branches", 6, 4, 512), ("merge_out", 4, 2, 1024),
    ("up2", 22, 8, 256), ("down2", 11, 2, 1024),
]
FIRST, COUNT, WIDTH, NK, COLS = {}, {}, [], {}, {}
for _name, _n, _k, _c in STREAM:
    FIRST[_name], COUNT[_name], NK[_name], COLS[_name] = len(WIDTH), _n, _k, _c
    WIDTH += [_k * _c] * _n
WIDTH[FIRST["mem_q"] + 2] = 2 * 520
UNITS = len(WIDTH)


def last(name):
    return FIRST[name] + COUNT[name]


GAINS = ["g_mem", "n00", "n01", "n02", "n03", "n10", "n11", "n12", "n13", "g_mix", "g_ffn"]


TAILS = ["even_out", "down0", "odd_out", "down1", "merge_out", "down2"]


def norm_count(g, t):
    return 2 * (g - g % 2) + g % 2 + 2 * t + 1 if 2 <= g <= 9 else 2 * g + t + 1


def half_count(g, t, i):
    return 2 * norm_count(g, t) - 1 + i


def constants():
    f = np.float32
    tok = np.arange(S, dtype=f)[:, None]
    inv = f(10000.0) ** (-np.arange(0, HD, 2, dtype=f) / f(HD))
    ang = tok * inv[None, :]
    inv2 = f(1.0) / (f(500000.0) ** (np.arange(8, dtype=f) * f(2.0) / f(16)))
    ang2 = tok * inv2[None, :]

    def by_tile(a):
        return a.reshape(NT, P, -1).transpose(1, 0, 2).reshape(P, -1)

    rope_a = np.concatenate([by_tile(np.cos(ang)), by_tile(np.sin(ang)), by_tile(-np.sin(ang))], 1)
    rope_m = np.concatenate([by_tile(np.cos(ang2)), by_tile(np.sin(ang2)), by_tile(-np.sin(ang2))], 1)
    q = np.arange(P)[:, None]
    k = np.arange(S)[None, :]

    def scores_mask(ok):
        return np.concatenate([np.where(ok(q, k[:, :P]), 0, MASKED), np.where(ok(q + P, k), 0, MASKED)], 1)

    window = scores_mask(lambda a, b: (b // CHUNK <= a // CHUNK) & (b // CHUNK >= a // CHUNK - 2))
    causal = scores_mask(lambda a, b: b <= a)
    m, l = np.arange(P)[:, None], np.arange(P)[None, :]
    block_causal = ((m // BLK == l // BLK) & (m <= l)).astype(np.uint32)
    keep = np.ones((P, S), f)
    keep[:, ::BLK] = 0
    pick = np.zeros((P, 8, P), f)
    for h in range(8):
        pick[h, h], pick[64 + h, h] = 1, 1
    return {
        "c_ident": np.eye(P, dtype=f), "c_rope_a": rope_a.astype(f), "c_rope_m": rope_m.astype(f),
        "c_window": window.astype(f), "c_causal": causal.astype(f), "c_block": block_causal,
        "c_keep": keep, "c_pick": pick.reshape(P, 8 * P),
    }


def lay_out(a):
    def rows(w, cols, k_of_unit):
        w = w[:, cols].reshape(-1, P, w[:, cols].shape[1])
        out = []
        for k0 in range(0, w.shape[0], k_of_unit):
            out.append(w[k0:k0 + k_of_unit].transpose(1, 0, 2).reshape(P, -1))
        return out

    def columns(w, groups):
        return [w[:, g].reshape(-1, P, len(g)).transpose(1, 0, 2).reshape(P, -1) for g in groups]

    r = np.arange
    pairs = [r(256 * j, 256 * j + 256) for j in range(4)]
    two = [np.concatenate([r(P * j, P * j + P), FF + r(P * j, P * j + P)]) for j in range(KF)]
    even, odd, w2 = a["even_w_in"][0], a["odd_w_in"][0], a["w_in_2"][0]
    u = rows(a["w_mem_kv_2"][0], r(1024), 2)
    heads = np.concatenate([r(HD * x, HD * x + HD) for p in range(4) for x in (p, 4 + p)] + [r(512, 768)])
    u += rows(even, heads, 2) + columns(even, [768 + g for g in pairs]) + rows(even, r(1792, 2816), 2)
    u += rows(a["even_w_out"][0], r(D), 2)
    u += columns(a["ffn_w_up"][0], two) + rows(a["ffn_w_down"][0], r(D), 2)
    for c in range(3):
        u += rows(odd, r(1024 * c, 1024 * c + 1024), 2)
    u += rows(a["odd_w_out"][0], r(D), 2)
    u += columns(a["ffn_w_up"][1], two) + rows(a["ffn_w_down"][1], r(D), 2)
    u += rows(w2, r(1024), 2) + rows(w2, np.concatenate([r(1024, 1536), r(2560, 3072)]), 2)
    u += rows(w2, r(1536, 2560), 2) + rows(w2, r(3072, 3592), 3)
    u += columns(w2, [3592 + r(256 * j, 256 * j + 256) for j in range(12)])
    for name in ("w_br_moba_2", "w_br_fox_2", "w_br_mem_2"):
        u += columns(a[name][0], [r(512), r(512, 1024)])
    u += rows(a["w_out_2"][0], r(D), 2)
    gate_up = np.concatenate([a["w_gate_2"][0], a["w_up_2"][0]], 1)
    u += columns(gate_up, two) + rows(a["w_down_2"][0], r(D), 2)
    weights = np.zeros((UNITS, P, UNIT), np.float32)
    for n, x in enumerate(u):
        weights[n, :, :x.shape[1]] = x
    nw = a["norm_w"]
    gains = np.stack([a["g_mem_2"][0], *nw[0], *nw[1], a["g_mix_2"][0], a["g_ffn_2"][0]])
    conv = np.concatenate([a["ffn_conv_w"], a["ffn_conv_b"][:, None]], 1)
    conv = conv.reshape(2, 4, KF, P).transpose(3, 0, 2, 1).reshape(P, 2 * KF * 4)
    head_gains = np.concatenate([a[x][0] for x in (
        "g_q_moba_2", "g_k_moba_2", "g_q_fox_2", "g_k_fox_2", "g_q_mem_2", "g_k_mem_2")])[None]
    rows_in = np.concatenate([a["even_sinks"][0], a["b_forget_2"][0]])[None]
    lb = a["hgrn_lb_logits"].reshape(2, HB, P).transpose(2, 0, 1).reshape(P, 2 * HB)
    table = np.pad(a["odd_rel_bias"][0][:, ::-1], ((0, 0), (127, 128)), mode="edge")
    table = np.stack([table[:, P - 1 - q:P - 1 - q + S] for q in range(P)], 1)
    table[:, :CHUNK, S - CHUNK:] = MASKED
    return {
        "weights": weights, "gains": gains, "conv": conv, "head_gains": head_gains, "rows_in": rows_in,
        "lb": lb, "hgrn_w": a["hgrn_norm_w"], "rel": table, "x": a["x"][0], "mem": a["mem_2"][0],
    }


def build(nc, dram, out):
    with ExitStack() as ctx:
        def sb(name, shape, dt=F32, stack=ctx):
            return stack.enter_context(nc.sbuf_tensor(name, [P, *shape], dt))

        sems = {}

        def sem(name):
            sems[name] = ctx.enter_context(nc.semaphore(name))
            return sems[name]

        with ExitStack() as r:
            lo = sb("lo", [RAW, UNIT], F32R, r)
        raw = sb("raw", [RAW, UNIT])
        hi = sb("hi", [RAW, UNIT], F32R)
        h = sb("h", [NT, D])
        y_hi = sb("y_hi", [KD, S], F32R)
        y_lo = sb("y_lo", [KD, S], F32R)
        gain = sb("gain", [2, D])
        xhat = sb("xhat", [NT, D])
        mk_t = sb("mk_t", [4, S])
        mv = sb("mv", [NT, 512])
        sc = sb("sc", [2, 512])
        pr = sb("pr", [2, 512])
        pt = sb("pt", [2, 512])
        ident = sb("ident", [P])
        rope_a = sb("rope_a", [3, NT, 32])
        rope_m = sb("rope_m", [3, NT, 8])
        causal = sb("causal", [384])
        block_causal = sb("block_causal", [P], U32)
        ones = sb("ones", [S])
        conv = sb("conv", [2, KF, 4])
        head_gain = sb("head_gain", [512])
        rows_in = sb("rows_in", [16])
        lb_in = sb("lb_in", [2, HB])
        lb = sb("lb", [2, HB])
        lb_d = sb("lb_d", [HB])
        half = sb("half", [16])
        warm = sb("warm", [16])
        ss = sb("ss", [2, 2, 2])
        ms = sb("ms", [2, 2])
        rstd = sb("rstd", [2, 2])
        hs = sb("hs", [2, 16])
        hm = sb("hm", [2, 16])
        hr = sb("hr", [2, 16])
        top = sb("top", [20, 2])
        neg = sb("neg", [20, 2])
        tot = sb("tot", [20, 2])
        rec = sb("rec", [20, 2])
        snk = sb("snk", [8, 2])
        esnk = sb("esnk", [8, 2])
        fz = sb("fz", [5, NT, 8])

        nlf = sb("nlf", [NT, P])
        ncum = sb("ncum", [S])
        pick = sb("pick", [8, P])

        with ExitStack() as r:
            h_hi = sb("h_hi", [KF, S], F32R, r)
            h_lo = sb("h_lo", [KF, S], F32R, r)
            gate = sb("gate", [24, S], F32, r)
        with ExitStack() as r:
            q_t = sb("q_t0", [4, S], F32, r)
            k_t = sb("k_t0", [S], F32, r)
            qk = sb("qk0", [NT, 640], F32, r)
            rot = sb("rot0", [640], F32, r)
            va = sb("va", [NT, P], F32, r)
            mk = sb("mk", [NT, 512], F32, r)
            hq = sb("hq", [HB, S], F32, r)
            hf = sb("hf", [HB, S], F32, r)
            hk = sb("hk", [HB, S], F32, r)
            hc = sb("hc", [HB, S], F32, r)
            he = sb("he", [HB, S], F32, r)
            hd = sb("hd", [HB, S], F32, r)
            kend = sb("kend", [NT, 512], F32, r)
            hv = sb("hv", [NT, 512], F32, r)
            hg = sb("hg", [NT, 512], F32, r)
            s_t = sb("s_t", [NT, HB, P], F32, r)
            state_own = sb("state_own", [3, HB, P], F32, r)
            hw = sb("hw", [512], F32, r)
            window = sb("window", [384], F32, r)
            keep = sb("keep", [S], F32, r)
        with ExitStack() as r:
            q1 = sb("q1", [NT, D], F32, r)
            k1 = sb("k1", [NT, D], F32, r)
            v1 = sb("v1", [NT, D], F32, r)
            q1_t = sb("q1_t", [8, S], F32, r)
            k1_t = sb("k1_t", [8, S], F32, r)
            bias = sb("bias", [4, S], F32, r)
            pt_all = sb("pt_all", [16, 384], F32, r)
        mem_x = k1
        with ExitStack() as r:
            qkm = sb("qkm", [NT, D], F32, r)
            qkf = sb("qkf", [NT, D], F32, r)
            v2 = sb("v2", [NT, D], F32, r)
            qkm_t = sb("qkm_t", [8, S], F32, r)
            qkf_t = sb("qkf_t", [8, S], F32, r)
            qc = sb("qc", [NT, 512], F32, r)
        ps = ctx.enter_context(nc.psum_tensor("ps", [P, 8, 512], F32))
        state = ([hf[:, 2 * i:2 * i + 2, :].rearrange("p a b -> p (a b)") for i in range(2)]
                 + [hk[:, 2 * i:2 * i + 2, :].rearrange("p a b -> p (a b)") for i in range(2)]
                 + [state_own[:, i].rearrange("p a b -> p (a b)") for i in range(3)])
        state = [s.rearrange("p (h e) -> p h e", h=HB) for s in state]
        qc_t = xhat[:, 0, :].rearrange("p (a b) -> p a b", a=4)
        m_sum = xhat[:, :, :].rearrange("p t n -> p (t n)").rearrange("p (k s) -> p k s", s=S)

        raw_in = [sem(f"raw_in{i}") for i in range(RAW)]
        const_in, ident_in = sem("const_in"), sem("ident_in")
        x_in, mem_in = sem("x_in"), [sem("mem_in0"), sem("mem_in1")]
        gain_in = [sem("gain_in0"), sem("gain_in1")]
        bias_in = [sem(f"bias_in{i}") for i in range(4)]
        out_in = sem("out_in")
        hi_done, lo_done = sem("hi_done"), sem("lo_done")
        unit_used = sem("unit_used")
        tile_done = sem("tile_done")
        set_up = sem("set_up")
        scaled_ms, rooted = sem("scaled_ms"), sem("rooted")
        squared, weighed, normed, resid = sem("squared"), sem("weighed"), sem("normed"), sem("resid")
        turned, y_hi_done, y_lo_done = sem("turned"), sem("y_hi_done"), sem("y_lo_done")
        head_sq, head_sum, head_ms, head_root = sem("head_sq"), sem("head_sum"), sem("head_ms"), sem("head_root")
        dve_link = sem("dve_link")
        scored, row_max, maxed, powed = sem("scored"), sem("row_max"), sem("maxed"), sem("powed")
        probs_turned, probs_copied, mixed = sem("probs_turned"), sem("probs_copied"), sem("mixed")
        first_mixed = sem("first_mixed")
        attended = sem("attended")
        conv_begun, conv_done, glued = sem("conv_begun"), sem("conv_done"), sem("glued")
        hmul, h_hi_done, h_lo_done = sem("hmul"), sem("h_hi_done"), sem("h_lo_done")
        mk_copied, mv_copied, hg_evac = sem("mk_copied"), sem("mv_copied"), sem("hg_evac")
        mk_ready, mk_turned, mk_evac = sem("mk_ready"), sem("mk_turned"), sem("mk_evac")
        dve_sink, act_sink = sem("dve_sink"), sem("act_sink")
        roped, a_turned, a_evac = sem("roped"), sem("a_turned"), sem("a_evac")
        lb_sub, lb_sig, lb_done = sem("lb_sub"), sem("lb_sig"), sem("lb_done")
        qf_evac, f_done, ln_done, cum_done = sem("qf_evac"), sem("f_done"), sem("ln_done"), sem("cum_done")
        exp_done, last_done, exp3_done, dec_done = sem("exp_done"), sem("last_done"), sem("exp3_done"), sem("dec_done")
        hv_evac, gated = sem("hv_evac"), sem("gated")
        kend_turned, kend_evac, st_made, st_evac = sem("kend_turned"), sem("kend_evac"), sem("st_made"), sem("st_evac")
        kv_made, stated, o_made, hgrn_out = sem("kv_made"), sem("stated"), sem("o_made"), sem("hgrn_out")
        q_evac, k_evac, v_evac, qk_turned, qk_evac = (sem(x) for x in ("q_evac", "k_evac", "v_evac", "qk_turned", "qk_evac"))
        m_evac, v2_evac, f_evac, c_evac = sem("m_evac"), sem("v2_evac"), sem("f_evac"), sem("c_evac")
        m_ready, f_ready, c_ready, nlf_ready = sem("m_ready"), sem("f_ready"), sem("c_ready"), sem("nlf_ready")
        forget, forget_e, forget_l = sem("forget"), sem("forget_e"), sem("forget_l")
        heads_turned, heads_evac = sem("heads_turned"), sem("heads_evac")
        k_copied, ncum_done, z_done = sem("k_copied"), sem("ncum_done"), sem("z_done")
        gate_evac, gate_sig = sem("gate_evac"), sem("gate_sig")
        br_turned, br_hi, br_lo, br_used = sem("br_turned"), sem("br_hi"), sem("br_lo"), sem("br_used")
        br_sum, merged_hi, merged_lo = sem("br_sum"), sem("merged_hi"), sem("merged_lo")

        block = ctx.enter_context(nc.Block())

        ATT = {"a": (0, 8, HD), "c": (8, 16, HD), "m": (24, 8, HD), "f": (32, 8, HD), "x": (40, 4, P)}
        COLUMN = {"a": 0, "c": 0, "m": 0, "f": 8, "x": 16}
        ATTENDED = {"a": 0, "c": 2, "m": 4, "f": 6, "x": 8}

        def third_heads(k):
            n = 2 * k
            return [("m", n), ("m", n + 1)] if n < 8 else [("f", n - 8), ("f", n - 7)] if n < 16 else [("x", n - 16), ("x", n - 15)]

        def branch_y(part, b, t):
            if b == 2:
                return (h_hi, h_lo)[part][:, 16:20, t * P:(t + 1) * P]
            return (y_hi, y_lo)[part][:, 4 * b:4 * b + 4, t * P:(t + 1) * P]

        FEATURE_MAJOR = (3, 6, 8)
        junk = [sc, pr]

        def each_tile(engine, tile):
            for r in range(4):
                tile(0, r)
            with engine.Fori(1, KF // 4) as i:
                for r in range(4):
                    tile(i, r)
            for r in range(KF % 4):
                tile(KF // 4, r)

        def whole(tile):
            return tile[:, :, :].rearrange("p a b -> p (a b)")

        def bank(b):
            return ps[:, b, :]

        def two_banks(b):
            return ps[:, b:b + 2, :].rearrange("p a b -> p (a b)")

        def split4(ap):
            return ap.rearrange("p (a b) -> p a b", a=4)

        def token_half(y, kh, t):
            return y[:, 4 * kh:4 * kh + 4, t * P:(t + 1) * P]

        @block.sync
        def _(sp):
            sp.dma_start(mem_x[:, 0, :], dram["mem"][0:P, :]).then_inc(mem_in[0], 16)
            sp.dma_start(ident[:, :], dram["c_ident"]).then_inc(ident_in, 16)
            for n in range(RAW):
                if n == 1:
                    sp.dma_start(mem_x[:, 1, :], dram["mem"][P:S, :]).then_inc(mem_in[1], 16)
                if n == 2:
                    sp.dma_start(h[:, :, :], dram["x"].rearrange("(t p) d -> p t d", p=P)).then_inc(x_in, 16)
                sp.dma_start(raw[:, n, :], dram["weights"][n]).then_inc(raw_in[n], 16)
            with sp.Fori(0, UNITS // RAW - 1) as i:
                for s in range(RAW):
                    sp.wait_ge(unit_used, RAW * i + s + 1)
                    sp.dma_start(raw[:, s, :], dram["weights"][RAW * i + (RAW + s)]).then_inc(raw_in[s], 16)
            for t in range(NT):
                sp.wait_ge(resid, 20 + 2 * t + 2)
                sp.dma_start(out[t * P:(t + 1) * P, :], h[:, t, :]).then_inc(out_in, 16)
            sp.wait_ge(out_in, 32)

        @block.gpsimd
        def _(pool):
            def gain_load(g):
                if g >= 2:
                    pool.wait_ge(weighed, half_count(g - 2, 1, 1))
                pool.dma_start(gain[:, g % 2, :], dram["gains"][g:g + 1, :].partition_broadcast(P)).then_inc(gain_in[g % 2], 16)

            pool.memset(half[:, :], -0.5).then_inc(set_up, 1)
            gain_load(0)
            gain_load(1)

            def root(*gains):
                for t in range(NT):
                    for g in gains:
                        n = norm_count(g, t)
                        if n == 1:
                            pool.wait_ge(set_up, 1)
                        pool.wait_ge(squared, 2 * n)
                        pool.tensor_scalar(ms[:, g % 2, t:t + 1], ss[:, g % 2, t, 0:1], ss[:, g % 2, t, 1:2], EPS, ALU.add, ALU.add).then_inc(scaled_ms, 1)
                        pool.wait_ge(scaled_ms, n)
                        pool.tensor_tensor(rstd[:, g % 2, t:t + 1], ms[:, g % 2, t:t + 1], half[:, 0:1], ALU.pow).then_inc(rooted, 1)

            def head_roots(i, nh, d):
                pool.wait_ge(head_sum, i + 1)
                pool.tensor_scalar(hm[:, i % 2, :nh], hs[:, i % 2, :nh], 1.0 / d, EPS, ALU.mult, ALU.add).then_inc(head_ms, 1)
                pool.wait_ge(head_ms, i + 1)
                pool.tensor_tensor(hr[:, i % 2, :nh], hm[:, i % 2, :nh], half[:, :nh], ALU.pow).then_inc(head_root, 1)

            root(0)
            root(1)
            loads = [
                (rope_a[:, :, :, :].rearrange("p a t f -> p (a t f)"), dram["c_rope_a"]),
                (rope_m[:, :, :, :].rearrange("p a t f -> p (a t f)"), dram["c_rope_m"]),
                (window[:, :], dram["c_window"]), (causal[:, :], dram["c_causal"]),
                (block_causal[:, :], dram["c_block"]), (keep[:, :], dram["c_keep"]),
                (pick[:, :, :].rearrange("p a b -> p (a b)"), dram["c_pick"]),
                (conv[:, :, :, :].rearrange("p a b c -> p (a b c)"), dram["conv"]),
                (head_gain[:, :], dram["head_gains"].partition_broadcast(P)),
                (rows_in[:, :], dram["rows_in"].partition_broadcast(P)),
                (lb_in[:, :, :].rearrange("p a b -> p (a b)"), dram["lb"]),
                (hw[:, :], dram["hgrn_w"].partition_broadcast(P)),
            ]
            for dst, src in loads:
                pool.dma_start(dst, src).then_inc(const_in, 16)
            pool.memset(ones[:, :], 1.0).then_inc(set_up, 1)
            pool.memset(s_t[:, :, :, :], 0.0).then_inc(set_up, 1)
            pool.memset(nlf[:, :, :], 0.0).then_inc(set_up, 1)
            gain_load(2)
            gain_load(3)
            for i in range(2):
                head_roots(i, 4, P)
            pool.wait_ge(const_in, 16 * 12)
            for t in range(NT):
                pool.wait_ge(hg_evac, t + 1)
                pool.tensor_tensor(hg[:, t, :], hg[:, t, :], hw[:, :], ALU.mult).then_inc(gated, 1)
            for i in range(2, 4):
                head_roots(i, 4, P)
            root(2, 3)
            gain_load(4)
            gain_load(5)
            root(4, 5)
            gain_load(6)
            gain_load(7)
            pool.wait_ge(q_evac, 2)
            for hh in range(16):
                if hh >= 4:
                    pool.wait_ge(row_max, ATT["c"][0] + hh - 3)
                pool.dma_start(bias[:, hh % 4, :], dram["rel"][hh]).then_inc(bias_in[hh % 4], 16)
            root(6, 7)
            gain_load(8)
            gain_load(9)
            root(8, 9)
            gain_load(10)
            for i in (4, 5, 6, 7):
                head_roots(i, 16, HD)
            for i in (8, 9):
                head_roots(i, 4, P)
            root(10)

        @block.scalar
        def _(act):
            done = [0]

            def round_unit(n, s=None, q=None, w=None):
                s, q = (n % RAW, n // RAW) if s is None else (s, q)
                act.wait_ge(raw_in[s], 16 * (q + 1))
                w = WIDTH[n] if w is None else w
                act.activation(hi[:, s, :w], raw[:, s, :w], ACT.Copy).then_inc(hi_done, 1)

            def units(upto):
                loops = (upto - done[0]) // RAW
                if loops >= 2:
                    n = done[0]
                    with act.Fori(0, loops) as i:
                        for s in range(RAW):
                            round_unit(RAW * i + (n + s), (n + s) % RAW, i + (n + s) // RAW, UNIT)
                    done[0] += RAW * loops
                while done[0] < upto:
                    round_unit(done[0])
                    done[0] += 1

            def round_part(parts, part):
                n, w = done[0], UNIT // parts
                c = slice(w * part, w * part + w)
                act.wait_ge(raw_in[n % RAW], 16 * (n // RAW + 1))
                ins = act.activation(hi[:, n % RAW, c], raw[:, n % RAW, c], ACT.Copy)
                if part == parts - 1:
                    ins.then_inc(hi_done, 1)
                    done[0] += 1

            def square(g, t, halves, waits):
                for i in range(2):
                    if g:
                        act.wait_ge(squared, 2 * norm_count(g, t) - 2)
                    act.wait_ge(*waits[i])
                    act.activation(junk[t][:, i, :], halves[i], ACT.Square, scale=D ** -0.5,
                                   accum_out=ss[:, g % 2, t, i:i + 1]).then_inc(squared, 1)

            def square_product(g, t, base, *ready):
                square(g, t, [bank(base + 2 * t), bank(base + 2 * t + 1)], [ready, (weighed, half_count(g, t, 0))])

            def square_tokens(g, t, src, *waits):
                square(g, t, [src[:, t, 0:512], src[:, t, 512:D]], waits)

            def square_sum(g, t, p):
                square_tokens(g, t, h, (resid, 4 * p + 2 * t + 1), (resid, 4 * p + 2 * t + 2))

            def turned_hi(stage, base, dst, tiles=(0, 1)):
                for t in tiles:
                    for kh in range(2):
                        act.wait_ge(turned, 4 * stage + 2 * t + kh + 1)
                        act.activation(token_half(dst, kh, t), split4(bank(base + 2 * t + kh)), ACT.Copy).then_inc(y_hi_done, 1)

            def norms_between(g, p, base, name, stage, turn_base):
                units(last(name) + 1)
                square_product(g, 0, base, tile_done, TAILS.index(name) + 1)
                units(last(name) + 2)
                square_sum(g + 1, 0, p)
                square_product(g, 1, base, unit_used, last(name))
                turned_hi(stage, turn_base, y_hi, (0,))
                square_sum(g + 1, 1, p)
                turned_hi(stage, turn_base, y_hi, (1,))

            def head_square(i, src, nh, d):
                if i >= 2:
                    act.wait_ge(head_sum, i - 1)
                act.activation(whole(junk[i % 2])[:, :nh * d].rearrange("p (a b) -> p a b", a=nh), src, ACT.Square).then_inc(head_sq, 1)

            def exps(stage, hh):
                a, col = ATT[stage][0] + hh, COLUMN[stage] + hh
                act.wait_ge(maxed, a + 1)
                if a >= 2:
                    act.wait_ge(probs_turned, a - 1)
                for t in range(NT):
                    c = slice(256 * t, 256 * t + 256) if stage == "x" else slice(P * t, P + 256 * t)
                    src = ps[:, a % 2, c] if stage == "x" else sc[:, a % 2, c]
                    e = act.activation(pr[:, a % 2, c], src, ACT.Exp, bias=neg[:, col, t:t + 1], accum_out=tot[:, col, t:t + 1])
                e.then_inc(powed, 1)

            def feed_forward(layer):
                up = FIRST[f"up{layer}"]
                J0 = KF * layer

                def copy(j, r):
                    act.wait_ge(hmul, J0 + j + 1)
                    act.activation(h_hi[:, j, :], pt[:, r % 2, :S], ACT.Copy).then_inc(h_hi_done, 1)

                def tile(i, r):
                    j = 4 * i + r
                    act.wait_ge(unit_used, j + up + 1)
                    if layer < 2:
                        act.activation(sc[:, r % 2, :S], ps[:, r, :S], ACT.Identity, scale=conv[:, layer, j, 2:3],
                                       bias=conv[:, layer, j, 3:4]).then_inc(conv_begun, 1)
                    if not (type(i) is int and j == 0):
                        copy(j - 1, r + 3)
                    round_unit(j + up + 2, (up + 2 + r) % RAW, i + (up + 2 + r) // RAW, UNIT)
                    if layer < 2:
                        act.wait_ge(conv_done, J0 + j + 1)
                        act.activation(pr[:, r % 2, :S], sc[:, r % 2, :S], ACT.Gelu).then_inc(glued, 1)
                    else:
                        act.activation(pr[:, r % 2, :S], ps[:, r, :S], ACT.Silu).then_inc(glued, 1)

                each_tile(act, tile)
                copy(KF - 1, KF - 1)
                done[0] += KF
                units(last(f"down{layer}"))

            square_tokens(0, 0, mem_x, (mem_in[0], 16), (mem_in[0], 16))
            units(1)
            turned_hi(0, 4, h_hi, (0,))
            square_tokens(0, 1, mem_x, (mem_in[1], 16), (mem_in[1], 16))
            units(2)
            turned_hi(0, 4, h_hi, (1,))
            for t in range(NT):
                square_tokens(1, t, h, (x_in, 16), (x_in, 16))
            units(FIRST["even_a"])
            turned_hi(1, 4, y_hi)
            units(FIRST["even_a"] + 1)
            act.wait_ge(unit_used, last("mem_kv"))
            for t in range(NT):
                act.activation(mk[:, t, :], bank(2 * t), ACT.Copy).then_inc(mk_copied, 1)
            units(FIRST["even_a"] + 2)
            for t in range(NT):
                act.wait_ge(mk_copied, t + 1)
                head_square(t, mk[:, t, :].rearrange("p (a b) -> p a b", a=4), 4, P)
            units(last("even_a") + 2)
            act.wait_ge(lb_sub, 1)
            act.activation(lb[:, 0, :], lb_d[:, :], ACT.Sigmoid).then_inc(lb_sig, 1)
            for u in range(4):
                act.wait_ge(unit_used, FIRST["even_qf"] + u + 1)
                dst = (hq if u < 2 else hf)[:, 2 * (u % 2):2 * (u % 2) + 2, :].rearrange("p a b -> p (a b)")
                act.activation(dst, bank(u), ACT.Copy if u < 2 else ACT.Sigmoid).then_inc(qf_evac, 1)
                units(FIRST["even_qf"] + u + 3)
            act.wait_ge(f_done, 1)
            act.activation(whole(hf), whole(hf), ACT.Ln).then_inc(ln_done, 1)
            units(FIRST["even_ig"] + 3)
            act.wait_ge(cum_done, 1)
            act.activation(whole(he), whole(hc), ACT.Exp).then_inc(exp_done, 1)
            act.activation(whole(hd), whole(hc), ACT.Exp, scale=-1.0).then_inc(exp_done, 1)
            units(FIRST["even_ig"] + 4)
            act.wait_ge(last_done, 1)
            act.activation(whole(hf), whole(hf), ACT.Exp).then_inc(exp3_done, 1)
            units(last("even_ig") + 1)
            act.wait_ge(unit_used, last("even_ig"))
            for t in range(NT):
                act.activation(hg[:, t, :], bank(4 + 2 * t + 1), ACT.Silu).then_inc(hg_evac, 1)
            units(last("even_ig") + 2)
            for b in range(2):
                act.wait_ge(a_turned, b + 1)
                act.activation(q_t[:, :, b * P:(b + 1) * P], split4(bank(b)), ACT.Copy, scale=HD ** -0.5).then_inc(a_evac, 1)
            act.wait_ge(a_turned, 3)
            act.activation(k_t[:, :], ps[:, 2, :S], ACT.Copy).then_inc(a_evac, 1)
            for t in range(NT):
                act.wait_ge(kend_turned, t + 1)
                act.activation(kend[:, t, :], bank(6 + t), ACT.Copy).then_inc(kend_evac, 1)
            for t in range(NT):
                act.wait_ge(o_made, t + 1)
                head_square(2 + t, split4(bank(4 + t)), 4, P)
            act.wait_ge(head_sum, 4)
            act.activation(warm[:, 8:16], half[:, 8:16], ACT.Exp)
            exps("a", 0)
            for t in range(NT):
                act.wait_ge(mk_turned, t + 1)
                act.activation(mk_t[:, :, t * P:(t + 1) * P], split4(bank(6 + t)), ACT.Copy).then_inc(mk_evac, 1)
            for hh in range(1, 8):
                exps("a", hh)
            act.wait_ge(maxed, 8)
            act.wait_ge(dve_sink, 1)
            act.activation(esnk[:, :, :], snk[:, :, :], ACT.Exp).then_inc(act_sink, 1)
            turned_hi(2, 4, y_hi)
            units(last("even_out"))
            norms_between(2, 0, 0, "even_out", 3, 4)
            feed_forward(0)
            norms_between(4, 1, 4, "down0", 4, 0)

            units(last("odd_q") + 2)
            act.wait_ge(unit_used, last("odd_q"))
            for t in range(NT):
                act.activation(q1[:, t, :], two_banks(4 + 2 * t), ACT.Copy).then_inc(q_evac, 1)
            units(last("odd_k") + 1)
            for b in range(4):
                act.wait_ge(qk_turned, b + 1)
                act.activation(token_half(q1_t, b % 2, b // 2), split4(bank(4 + b)), ACT.Copy, scale=HD ** -0.5).then_inc(qk_evac, 1)
            act.wait_ge(unit_used, last("odd_k"))
            act.activation(k1[:, 0, :], two_banks(0), ACT.Copy).then_inc(k_evac, 1)
            units(last("odd_k") + 2)
            for b in range(2):
                act.wait_ge(qk_turned, 4 + b + 1)
                act.activation(token_half(k1_t, b % 2, b // 2), split4(bank(b)), ACT.Copy).then_inc(qk_evac, 1)
            units(last("odd_v"))
            for hh in range(16):
                round_part(4, hh % 4)
                if hh == 8:
                    act.wait_ge(unit_used, last("odd_v"))
                    act.activation(v1[:, 0, :], two_banks(4), ACT.Copy).then_inc(v_evac, 1)
                exps("c", hh)
            turned_hi(5, 0, y_hi)
            units(last("odd_out"))
            norms_between(6, 2, 4, "odd_out", 6, 4)
            feed_forward(1)
            norms_between(8, 3, 4, "down1", 7, 0)

            units(last("moba_qk") + 1)
            act.wait_ge(unit_used, last("moba_qk"))
            act.activation(qkm[:, 0, :], two_banks(4), ACT.Copy).then_inc(m_evac, 1)
            units(last("moba_qk") + 2)
            act.wait_ge(m_evac, 2)
            for t in range(NT):
                head_square(4 + t, qkm[:, t, :].rearrange("p (a b) -> p a b", a=16), 16, HD)
            units(last("both_v") + 1)
            act.wait_ge(unit_used, last("both_v"))
            act.activation(v2[:, 0, :], two_banks(0), ACT.Copy).then_inc(v2_evac, 1)
            units(last("fox_qk") + 1)
            act.wait_ge(unit_used, last("fox_qk"))
            act.activation(qkf[:, 0, :], two_banks(4), ACT.Copy).then_inc(f_evac, 1)
            units(last("fox_qk") + 2)
            act.wait_ge(f_evac, 2)
            for t in range(NT):
                act.wait_ge(head_sum, 5 + t)
                head_square(6 + t, qkf[:, t, :].rearrange("p (a b) -> p a b", a=16), 16, HD)
            units(last("mem_q") + 1)
            act.wait_ge(unit_used, last("mem_q"))
            for t in range(NT):
                act.activation(qc[:, t, :], bank(2 * t + 1), ACT.Copy).then_inc(c_evac, 1)
            units(last("mem_q") + 2)
            for t in range(NT):
                act.wait_ge(head_sum, 7 + t)
                act.wait_ge(c_evac, t + 1)
                head_square(8 + t, qc[:, t, :].rearrange("p (a b) -> p a b", a=4), 4, P)
            act.wait_ge(forget, 1)
            act.activation(fz[:, 2, :, :], fz[:, 1, :, :], ACT.Exp, scale=-1.0).then_inc(forget_e, 1)
            act.wait_ge(forget_e, 1)
            act.activation(fz[:, 3, :, :], fz[:, 2, :, :], ACT.Ln, bias=1.0).then_inc(forget_l, 1)

            def gate_copy(u):
                act.wait_ge(unit_used, FIRST["gates"] + u + 1)
                act.activation(gate[:, 2 * u:2 * u + 2, :].rearrange("p a b -> p (a b)"), bank(6 + u % 2), ACT.Copy).then_inc(gate_evac, 1)

            def heads_copy(first, n, dst, q_tiles, base):
                for b in range(n):
                    kh, t = b % 2, b // 2
                    act.wait_ge(heads_turned, first + b + 1)
                    act.activation(token_half(dst, kh, t), split4(bank(base + b)), ACT.Copy,
                                   scale=HD ** -0.5 if kh == 0 else 1.0).then_inc(heads_evac, 1)

            heads_copy(0, 4, qkm_t, 4, 2)
            gate_copy(0)
            units(FIRST["gates"] + 3)
            heads_copy(4, 4, qkf_t, 4, 2)
            gate_copy(1)
            for t in range(NT):
                act.wait_ge(heads_turned, 8 + t + 1)
                act.activation(qc_t[:, :, t * P:(t + 1) * P], split4(bank(2 + t)), ACT.Copy, scale=P ** -0.5).then_inc(heads_evac, 1)
            for k in range(10):
                units(FIRST["gates"] + k + 4)
                for stage, hh in third_heads(k):
                    exps(stage, hh)
                if k >= 1:
                    gate_copy(k + 1)
            gate_copy(11)
            for b in range(6):
                act.wait_ge(br_turned, b + 1)
                act.activation(branch_y(0, b // 2, b % 2), split4(bank(b)), ACT.Copy).then_inc(br_hi, 1)
            act.wait_ge(gate_evac, 12)
            for b in range(3):
                units(FIRST["branches"] + b + 2)
                g = gate[:, 8 * b:8 * b + 8, :].rearrange("p a b -> p (a b)")
                act.activation(g, g, ACT.Sigmoid).then_inc(gate_sig, 1)
            units(FIRST["merge_out"] + 2)
            for c in range(2):
                act.wait_ge(br_sum, 2 + c + 1)
                act.activation(h_hi[:, 4 * c:4 * c + 4, :], m_sum[:, 4 * c:4 * c + 4, :], ACT.Copy).then_inc(merged_hi, 1)
            units(last("merge_out"))
            square_sum(10, 0, 4)
            units(last("merge_out") + 1)
            square_sum(10, 1, 4)
            turned_hi(8, 4, y_hi)
            units(last("merge_out") + 2)
            feed_forward(2)
            assert done[0] == UNITS

        @block.tensor
        def _(pe):
            def wait_unit(n):
                pe.wait_ge(lo_done, n + 1)

            def tokens_unit(name, n, k, t, base, y, splits):
                yh, yl = y
                cols, total = COLS[name], sum(WIDTH[FIRST[name]:last(name)]) // COLS[name]
                tok = slice(t * P, (t + 1) * P)
                for kk in range(WIDTH[n] // cols):
                    for x, w, first, final in ((yh, hi, True, False), (yh, lo, False, False), (yl, hi, False, True)):
                        for half_, (c0, cw) in enumerate(splits):
                            mm = pe.matmul(ps[:, base + 2 * t + half_, :cw], x[:, k + kk, tok],
                                           w[:, n % RAW, kk * cols + c0:kk * cols + c0 + cw],
                                           start=first and k + kk == 0, stop=final and k + kk == total - 1)
                return mm

            def tokens_by(name, base, y, splits=((0, 512), (512, 512)), entry=None, ready=None, before_last=lambda: None, needs=None):
                n0, n1 = FIRST[name], last(name)
                first_k = [sum(WIDTH[n0:n]) // COLS[name] for n in range(n0, n1)]

                def part(n, t):
                    return tokens_unit(name, n, first_k[n - n0], t, base, y, splits)

                def pair(n, between=lambda: None, halfway=lambda mm: None):
                    wait_unit(n)
                    part(n, 0)
                    between()
                    wait_unit(n + 1)
                    halfway(part(n + 1, 0))
                    for m in (n, n + 1):
                        if ready is not None and m == n0:
                            pe.wait_ge(*ready)
                        part(m, 1).then_inc(unit_used, 1)

                n = n0
                if entry is not None:
                    pair(n, lambda: entry(1))
                    n += 2
                    pe.wait_ge(ready[0], ready[1] + 1)
                tail = n1 - 2 if name in TAILS else n1
                while n < tail:
                    if n == n1 - 1:
                        before_last()
                    wait_unit(n)
                    if needs is not None:
                        pe.wait_ge(*needs(n - n0))
                    part(n, 0)
                    part(n, 1).then_inc(unit_used, 1)
                    n += 1
                if name in TAILS:
                    if needs is not None:
                        pe.wait_ge(*needs(n + 1 - n0))
                    pair(n, halfway=lambda mm: mm.then_inc(tile_done, 1))

            def features_of(n, s, outs, y, nk=KD, cols=256, stage=None):
                pe.wait_ge(lo_done, n + 1)
                yh, yl = y
                for f, dst in enumerate(outs):
                    for k in range(nk):
                        if stage is not None and f == 0 and k % 4 == 0:
                            pe.wait_ge(y_lo_done, 4 * stage + 3 + k // 4)
                        at = slice(k * cols + f * P, k * cols + (f + 1) * P)
                        for w, x, first, final in ((hi, yh, True, False), (hi, yl, False, False), (lo, yh, False, True)):
                            mm = pe.matmul(dst, w[:, s % RAW, at], x(k), start=first and k == 0, stop=final and k == nk - 1)
                return mm

            def of_tiles(y):
                return tuple((lambda k, part=part: part[:, k, :]) for part in y)

            def turn(stage, src, base, t, ready, count):
                for kh in range(2):
                    pe.wait_ge(ready, 2 * count - 1 + kh if ready is normed else count)
                    for kk in range(4):
                        mm = pe.transpose(ps[:, base + 2 * t + kh, kk * P:(kk + 1) * P],
                                          src[:, t, (4 * kh + kk) * P:(4 * kh + kk + 1) * P], ident[:, :])
                    mm.then_inc(turned, 1)

            def enter(stage, base, name, out_base, ready=normed, counts=None, y=None, before_last=lambda: None):
                counts = counts or [2 * NORM_OF_TURN[stage] + 1, 2 * NORM_OF_TURN[stage] + 2]
                turn(stage, xhat, base, 0, ready, counts[0])
                pe.wait_ge(y_lo_done, 4 * stage + 1)
                tokens_by(name, out_base, y or Y, entry=lambda t: turn(stage, xhat, base, t, ready, counts[1]),
                          ready=(y_lo_done, 4 * stage + 3), before_last=before_last)

            NORM_OF_TURN = {0: 0, 1: 1, 3: 2, 4: 3, 6: 4, 7: 5, 8: 6}

            def turn_heads(src, t, c0, b, signal, n=4):
                for kk in range(n):
                    mm = pe.transpose(ps[:, b, kk * P:(kk + 1) * P], src[:, t, c0 + kk * P:c0 + (kk + 1) * P], ident[:, :])
                mm.then_inc(signal, 1)

            def operands(stage, hh):
                if stage == "a":
                    g, p = hh // 4, hh % 4
                    r = slice(64 * g, 64 * g + 64)
                    return q_t[r, p, :], k_t[r, :], lambda kt: va[:, kt, 64 * g:64 * g + 64]
                if stage == "x":
                    return qc_t[:, hh, :], mk_t[:, hh, :], lambda kt: mv[:, kt, hh * P:(hh + 1) * P]
                r = slice(64 * (hh % 2), 64 * (hh % 2) + 64)
                if stage == "c":
                    return q1_t[r, hh // 2, :], k1_t[r, hh // 2, :], None
                tile = qkm_t if stage == "m" else qkf_t
                off = 0 if stage == "m" else 512
                return tile[r, hh // 2, :], tile[r, 4 + hh // 2, :], lambda kt: v2[:, kt, off + hh * HD:off + (hh + 1) * HD]

            def place(stage, hh, t):
                if stage == "c":
                    return ps[:, 4 + 2 * t + hh // 8, (hh % 8) * HD:(hh % 8 + 1) * HD]
                d = ATT[stage][2]
                return ps[:, 4 + t, hh * d:(hh + 1) * d]

            def scores(stage, hh):
                a = ATT[stage][0] + hh
                q, k, _ = operands(stage, hh)
                if a >= 2:
                    pe.wait_ge(powed if stage == "x" and hh >= 2 else row_max, a - 1)
                for t in range(NT):
                    n = S if stage == "x" else P * (t + 1)
                    c0 = S * t if stage == "x" else P * t
                    dst = ps[:, a % 2, c0:c0 + n]
                    mm = pe.matmul(dst, q[:, t * P:(t + 1) * P], k[:, :n], start=True, stop=stage != "f")
                    if stage == "f":
                        r = slice(64 * (hh % 2), 64 * (hh % 2) + 64)
                        mm = pe.matmul(dst, pick[r, hh, :], ncum[r, :n], start=False, stop=True)
                mm.then_inc(scored, 1)

            def turn_probs(stage, hh):
                a = ATT[stage][0] + hh
                pe.wait_ge(powed, a + 1)
                if a >= 2:
                    pe.wait_ge(probs_copied, a - 1)
                for i in range(4 if stage == "x" else 3):
                    mm = pe.transpose(ps[:, 2 + a % 2, i * P:(i + 1) * P], pr[:, a % 2, i * P:(i + 1) * P], ident[:, :])
                mm.then_inc(probs_turned, 1)

            def mix(stage, hh):
                a = ATT[stage][0] + hh
                _, _, v = operands(stage, hh)
                pe.wait_ge(probs_copied, a + 1)
                i = 0
                for t in range(NT):
                    kts = range(2 if stage == "x" else t + 1)
                    for kt in kts:
                        mm = pe.matmul(place(stage, hh, t), pt[:, a % 2, i * P:(i + 1) * P], v(kt),
                                       start=kt == 0, stop=kt == kts[-1])
                        i += 1
                mm.then_inc(mixed, 1)

            Y = (y_hi, y_lo)
            pe.wait_ge(ident_in, 16)
            enter(0, 4, "mem_kv", 0, y=(h_hi, h_lo), before_last=lambda: [turn(1, xhat, 4, t, normed, 3 + t) for t in range(NT)])
            pe.wait_ge(y_lo_done, 8)
            tokens_by("even_a", 4, Y, ((0, 512), (512, 256)))
            pe.wait_ge(mk_copied, 2)
            pe.wait_ge(mv_copied, 2)
            for u in range(4):
                n = FIRST["even_qf"] + u
                features_of(n, n % RAW, [ps[:, u, f * S:(f + 1) * S] for f in range(2)], of_tiles(Y)).then_inc(unit_used, 1)
            pe.wait_ge(roped, 2)
            tokens_by("even_ig", 4, Y)
            pe.wait_ge(qf_evac, 4)
            for t in range(NT):
                for p in range(4):
                    mm = pe.transpose(ps[:, t, p * P:(p + 1) * P],
                                      qk[:, t, p * P:(p + 1) * P], ident[:, :])
                mm.then_inc(a_turned, 1)
            for t in range(NT):
                mm = pe.transpose(ps[:, 2, t * P:(t + 1) * P], qk[:, t, 512:640], ident[:, :])
            mm.then_inc(a_turned, 1)
            pe.wait_ge(hg_evac, 2)
            pe.wait_ge(hv_evac, 2)
            pe.wait_ge(dec_done, 3)
            for t in range(NT):
                for hh in range(HB):
                    mm = pe.transpose(ps[:, 6 + t, hh * P:(hh + 1) * P], hc[:, hh, t * P:(t + 1) * P], ident[:, :])
                mm.then_inc(kend_turned, 1)
            for t in range(NT):
                tok = slice(t * P, (t + 1) * P)
                for hh in range(HB):
                    mm = pe.matmul(ps[:, 3 + t, hh * P:(hh + 1) * P], hd[:, hh, tok], hq[:, hh, tok], start=True, stop=True)
                mm.then_inc(st_made, 1)
            pe.wait_ge(kend_evac, 2)
            for b in range(NBLK - 1):
                if b >= 3:
                    pe.wait_ge(stated, b - 2)
                r = slice(BLK * (b % 4), BLK * (b % 4) + BLK)
                for hh in range(HB):
                    mm = pe.matmul(ps[:, 5 + b % 3, hh * P:(hh + 1) * P], kend[r, b // 4, hh * P:(hh + 1) * P],
                                   hv[r, b // 4, hh * P:(hh + 1) * P], start=True, stop=True)
                mm.then_inc(kv_made, 1)
            pe.wait_ge(st_evac, 2)
            for t in range(NT):
                pe.wait_ge(stated, 3 + 4 * t)
                for hh in range(HB):
                    cols = slice(hh * P, (hh + 1) * P)
                    mm = pe.matmul(ps[:, 4 + t, cols], s_t[:, t, hh, :], hv[:, t, cols], start=True, stop=True, skip_group_check=True)
                    for b in range(max(4 * t, 1), 4 * t + 4):
                        j = b % 4
                        mm = pe.matmul(ps[BLK * j:BLK * j + BLK, 4 + t, cols], hq[:, hh, b * BLK:(b + 1) * BLK],
                                       state[b - 1][:, hh, :], start=False, stop=True, skip_group_check=True)
                mm.then_inc(o_made, 1)
            pe.wait_ge(a_evac, 3)
            scores("a", 0)
            scores("a", 1)
            pe.wait_ge(mk_ready, 2)
            for t in range(NT):
                turn_heads(mk, t, 0, 6 + t, mk_turned)
            for i in range(2, 11):
                if i < 8:
                    scores("a", i)
                if i < 10:
                    turn_probs("a", i - 2)
                if i == 3:
                    pe.wait_ge(hgrn_out, 2)
                if i >= 3:
                    mix("a", i - 3)
            pe.wait_ge(mk_evac, 2)
            enter(2, 4, "even_out", 0, attended, [2, 2])

            def feed_forward(layer, stage, base):
                up = FIRST[f"up{layer}"]

                for t in range(NT):
                    turn(stage, xhat, base, t, normed, 2 * NORM_OF_TURN[stage] + t + 1)

                def tile(i, r):
                    j = 4 * i + r
                    if not (type(i) is int and i == 0):
                        pe.wait_ge(hmul, j + (KF * layer - 3))
                    features_of(j + up, (up + r) % RAW, [ps[:, r, f * S:(f + 1) * S] for f in range(2)], of_tiles(Y),
                                stage=stage if type(i) is int and j == 0 else None).then_inc(unit_used, 1)

                each_tile(pe, tile)
                tokens_by(f"down{layer}", 4, (h_hi, h_lo), needs=lambda u: (h_lo_done, KF * layer + 2 * u + 2))

            feed_forward(0, 3, 4)
            enter(4, 0, "odd_q", 4)
            def turn_q():
                pe.wait_ge(q_evac, 2)
                for b in range(4):
                    turn_heads(q1, b // 2, 512 * (b % 2), 4 + b, qk_turned)

            tokens_by("odd_k", 0, Y, before_last=turn_q)

            v_steps = [(n, kk, t, c) for n in range(FIRST["odd_v"], last("odd_v")) for kk in range(2) for t in range(NT) for c in range(2)]

            def v_step(i):
                n, kk, t, c = v_steps[i]
                k = 2 * (n - FIRST["odd_v"]) + kk
                if i % 8 == 0:
                    wait_unit(n)
                for x, w, first, final in ((y_hi, hi, True, False), (y_hi, lo, False, False), (y_lo, hi, False, True)):
                    mm = pe.matmul(ps[:, 4 + 2 * t + c, :], x[:, k, t * P:(t + 1) * P],
                                   w[:, n % RAW, kk * D + 512 * c:kk * D + 512 * c + 512], start=first and k == 0, stop=final and k == KD - 1)
                if i % 8 == 7:
                    mm.then_inc(unit_used, 1)

            pe.wait_ge(qk_evac, 4)
            for i in range(8):
                v_step(i)
            pe.wait_ge(k_evac, 2)
            for b in range(4):
                turn_heads(k1, b // 2, 512 * (b % 2), b, qk_turned)
            for i in range(8, 16):
                v_step(i)
            pe.wait_ge(qk_evac, 6)
            pe.wait_ge(k_copied, 2)

            def mix_tile(hh, t):
                for kt in range(t + 1):
                    mm = pe.matmul(place("c", hh, t), pt_all[:, hh, (t + kt) * P:(t + kt + 1) * P], v1[:, kt, hh * HD:(hh + 1) * HD],
                                   start=kt == 0, stop=kt == t)
                return mm

            for i in range(17):
                if i < 16:
                    scores("c", i)
                if i < 8:
                    v_step(16 + 2 * i)
                    v_step(17 + 2 * i)
                if i >= 1:
                    turn_probs("c", i - 1)
                if 9 <= i < 16:
                    if i == 9:
                        pe.wait_ge(v_evac, 2)
                    for hh in (2 * (i - 9), 2 * (i - 9) + 1):
                        pe.wait_ge(probs_copied, ATT["c"][0] + hh + 1)
                        mix_tile(hh, 0)
                        mix_tile(hh, 1).then_inc(mixed, 1)
            pe.wait_ge(probs_copied, 24)
            mix_tile(14, 0)
            mix_tile(15, 0).then_inc(first_mixed, 1)
            for hh in (14, 15):
                mix_tile(hh, 1).then_inc(mixed, 1)
            enter(5, 0, "odd_out", 4, attended, [3, 4])
            feed_forward(1, 6, 4)
            enter(7, 0, "moba_qk", 4)
            tokens_by("both_v", 0, Y)
            pe.wait_ge(m_evac, 2)
            tokens_by("fox_qk", 4, Y)
            pe.wait_ge(v2_evac, 2)
            tokens_by("mem_q", 0, Y, ((0, 8), (8, 512)))

            def gate_unit(u):
                n = FIRST["gates"] + u
                if u >= 2:
                    pe.wait_ge(gate_evac, u - 1)
                features_of(n, n % RAW, [ps[:, 6 + u % 2, f * S:(f + 1) * S] for f in range(2)], of_tiles(Y)).then_inc(unit_used, 1)

            pe.wait_ge(c_evac, 2)
            pe.wait_ge(z_done, 2)
            pe.wait_ge(f_evac, 2)
            for b in range(4):
                pe.wait_ge(m_ready, b // 2 + 1)
                turn_heads(qkm, b // 2, 512 * (b % 2), 2 + b, heads_turned)
            gate_unit(0)
            pe.wait_ge(heads_evac, 4)
            for b in range(4):
                pe.wait_ge(f_ready, b // 2 + 1)
                turn_heads(qkf, b // 2, 512 * (b % 2), 2 + b, heads_turned)
            gate_unit(1)
            pe.wait_ge(heads_evac, 8)
            for t in range(NT):
                pe.wait_ge(c_ready, t + 1)
                turn_heads(qc, t, 0, 2 + t, heads_turned)
            pe.wait_ge(nlf_ready, 1)
            for t in range(NT):
                mm = pe.transpose(ps[:, 4, t * P:(t + 1) * P], nlf[:, t, :], ident[:, :])
            mm.then_inc(heads_turned, 1)
            pe.wait_ge(heads_evac, 10)
            pe.wait_ge(ncum_done, 1)
            for k in range(10):
                now, before = third_heads(k), third_heads(k - 1) if k else []
                for stage, hh in now:
                    scores(stage, hh)
                for stage, hh in before:
                    if hh == 0 and stage != "m":
                        pe.wait_ge(attended, ATTENDED[stage])
                    mix(stage, hh)
                gate_unit(k + 2)
                for stage, hh in now:
                    turn_probs(stage, hh)
            for stage, hh in third_heads(9):
                mix(stage, hh)
            pe.wait_ge(gate_evac, 12)
            for b in range(6):
                pe.wait_ge(attended, 4 + b + 1)
                turn_heads((qkm, qkf, qkm)[b // 2], b % 2, 512 * (b // 4), b, br_turned)
            for u in range(6):
                n = FIRST["branches"] + u
                b = u // 2
                pe.wait_ge(br_lo, (2, 4, 4, 4, 6, 6)[u])
                if u >= 2:
                    pe.wait_ge(br_used, u - 1)
                if b == 2:
                    ys = tuple((lambda k, part=part: part[:, 16 + k, :]) for part in (h_hi, h_lo))
                else:
                    ys = tuple((lambda k, part=part: part[:, 4 * b + k, :]) for part in Y)
                outs = [ps[:, 2 * (u % 2) + f // 2, (f % 2) * S:(f % 2 + 1) * S] for f in range(4)]
                features_of(n, n % RAW, outs, ys, 4, 512).then_inc(unit_used, 1)
            tokens_by("merge_out", 4, (h_hi, h_lo), needs=lambda u: (merged_lo, u // 2 + 1))
            feed_forward(2, 8, 4)

        @block.vector
        def _(dve):
            done, links = [0], [0]

            def split_unit(n, s=None, w=None):
                s = n % RAW if s is None else s
                w = WIDTH[n] if w is None else w
                dve.wait_ge(hi_done, n + 1)
                dve.tensor_tensor(lo[:, s, :w], raw[:, s, :w], hi[:, s, :w].bitcast(F32), ALU.subtract).then_inc(lo_done, 1)

            def units(upto):
                loops = (upto - done[0]) // RAW
                if loops >= 2:
                    n = done[0]
                    with dve.Fori(0, loops) as i:
                        for s in range(RAW):
                            split_unit(RAW * i + (n + s), (n + s) % RAW, UNIT)
                    done[0] += RAW * loops
                while done[0] < upto:
                    split_unit(done[0])
                    done[0] += 1

            def split_part(parts, part):
                n, w = done[0], UNIT // parts
                c = slice(w * part, w * part + w)
                dve.wait_ge(hi_done, n + 1)
                ins = dve.tensor_tensor(lo[:, n % RAW, c], raw[:, n % RAW, c], hi[:, n % RAW, c].bitcast(F32), ALU.subtract)
                if part == parts - 1:
                    ins.then_inc(lo_done, 1)
                    done[0] += 1

            def link(ins):
                links[0] += 1
                ins.then_inc(dve_link, 1)
                dve.wait_ge(dve_link, links[0])

            def gain_wait(g):
                dve.wait_ge(gain_in[g % 2], 16 * (g // 2 + 1))

            def weigh(g, t, halves, order=(0, 1), waits=None):
                if t == 0:
                    gain_wait(g)
                for i, c in enumerate(order):
                    if waits is not None:
                        dve.wait_ge(*waits[i])
                    cols = slice(512 * c, 512 * c + 512)
                    dve.tensor_tensor(xhat[:, t, cols], halves[c], gain[:, g % 2, cols], ALU.mult).then_inc(weighed, 1)

            def norm(g, r, t, src):
                if r == 1:
                    dve.wait_ge(turned, 2 * t + 2)
                weigh(g, t, [src[:, t, 0:512], src[:, t, 512:D]])
                scale(g, t)

            def scale(g, t):
                dve.wait_ge(rooted, norm_count(g, t))
                for c in range(2):
                    dve.wait_ge(weighed, half_count(g, t, c))
                    cols = slice(512 * c, 512 * c + 512)
                    dve.tensor_scalar(xhat[:, t, cols], xhat[:, t, cols], rstd[:, g % 2, t:t + 1], None, ALU.mult).then_inc(normed, 1)

            def turned_lo(stage, base, dst, dst_hi, tiles=(0, 1)):
                for t in tiles:
                    for kh in range(2):
                        dve.wait_ge(y_hi_done, 4 * stage + 2 * t + kh + 1)
                        dve.tensor_tensor(token_half(dst, kh, t), split4(bank(base + 2 * t + kh)),
                                          token_half(dst_hi, kh, t).bitcast(F32), ALU.subtract).then_inc(y_lo_done, 1)

            def weigh_product(g, t, base, *ready):
                weigh(g, t, [bank(base + 2 * t), bank(base + 2 * t + 1)], (1, 0), [ready, (squared, half_count(g, t, 0))])

            def add_product(g, p, t):
                dve.wait_ge(weighed, half_count(g, t, 1))
                dve.wait_ge(rooted, norm_count(g, t))
                for c in range(2):
                    cols = slice(512 * c, 512 * c + 512)
                    dve.scalar_tensor_tensor(h[:, t, cols], xhat[:, t, cols], rstd[:, g % 2, t:t + 1], h[:, t, cols],
                                             ALU.mult, ALU.add).then_inc(resid, 1)
                dve.wait_ge(resid, 4 * p + 2 * t + 2)

            def norms_between(g, p, base, name, stage, turn_base, r):
                dve.wait_ge(turned, 4 * stage)
                weigh_product(g, 0, base, tile_done, TAILS.index(name) + 1)
                units(last(name) + 1)
                add_product(g, p, 0)
                weigh(g + 1, 0, [h[:, 0, 0:512], h[:, 0, 512:D]])
                weigh_product(g, 1, base, unit_used, last(name))
                scale(g + 1, 0)
                if stage in FEATURE_MAJOR:
                    add_product(g, p, 1)
                    weigh(g + 1, 1, [h[:, 1, 0:512], h[:, 1, 512:D]])
                    turned_lo(stage, turn_base, y_lo, y_hi, (0,))
                    scale(g + 1, 1)
                    turned_lo(stage, turn_base, y_lo, y_hi, (1,))
                    units(last(name) + 2)
                else:
                    turned_lo(stage, turn_base, y_lo, y_hi, (0,))
                    units(last(name) + 2)
                    add_product(g, p, 1)
                    norm(g + 1, r, 1, h)
                    turned_lo(stage, turn_base, y_lo, y_hi, (1,))

            def add_residual(name, base, t):
                dve.wait_ge(*((tile_done, TAILS.index(name) + 1) if t == 0 else (unit_used, last(name))))
                for c in range(2):
                    cols = slice(512 * c, 512 * c + 512)
                    dve.tensor_tensor(h[:, t, cols], bank(base + 2 * t + c), h[:, t, cols], ALU.add).then_inc(resid, 1)
                dve.wait_ge(resid, 4 * (4 + (name == "down2")) + 2 * t + 2)

            def head_sums(i, nh, d):
                dve.wait_ge(head_sq, i + 1)
                dve.tensor_reduce(hs[:, i % 2, :nh], whole(junk[i % 2])[:, :nh * d].rearrange("p (a b) -> p a b", a=nh),
                                  AX.X, ALU.add).then_inc(head_sum, 1)

            def head_scale(i, out_, src, nh, d):
                dve.wait_ge(head_root, i + 1)
                link(dve.tensor_tensor(out_, src, hr[:, i % 2, :nh].rearrange("p (a b) -> p a b", b=1).to_broadcast([P, nh, d]), ALU.mult))

            def head_gains(out_, nh, d, off):
                g = head_gain[:, off:off + d].rearrange("p (a b) -> p a b", a=1).to_broadcast([P, nh, d])
                return dve.tensor_tensor(out_, out_, g, ALU.mult)

            def heads_view(ap, d):
                return ap.rearrange("p (a b) -> p a b", b=d)

            def scores_max(stage, hh):
                a, col = ATT[stage][0] + hh, COLUMN[stage] + hh
                dve.wait_ge(scored, a + 1)
                if a >= 2:
                    dve.wait_ge(powed, a - 1)
                if stage == "x":
                    dve.tensor_reduce(top[:, col, :], ps[:, a % 2, :].rearrange("p (t k) -> p t k", t=NT), AX.X, ALU.max).then_inc(row_max, 1)
                else:
                    if stage == "c":
                        dve.wait_ge(bias_in[hh % 4], 16 * (hh // 4 + 1))
                    for t in range(NT):
                        c = slice(P * t, P + S * t)
                        add = {"a": window[:, c], "m": causal[:, c], "f": causal[:, c]}.get(stage)
                        if stage == "c":
                            add = bias[:, hh % 4, (P if t == 0 else 0):S]
                        init = rows_in[:, hh:hh + 1] if stage == "a" else MASKED
                        ins = dve.tensor_tensor_reduce(sc[:, a % 2, c], ps[:, a % 2, c], add, 1.0, init, ALU.add, ALU.max,
                                                       top[:, col, t:t + 1])
                    ins.then_inc(row_max, 1)
                dve.wait_ge(row_max, a + 1)
                dve.tensor_scalar(neg[:, col, :], top[:, col, :], -1.0, None, ALU.mult).then_inc(maxed, 1)

            def probs_copy(stage, hh):
                a = ATT[stage][0] + hh
                n = 512 if stage == "x" else 384
                dst = pt_all[:, hh, :] if stage == "c" else pt[:, a % 2, :n]
                dve.wait_ge(probs_turned, a + 1)
                if a >= 2 and stage != "c":
                    dve.wait_ge(mixed, a - 1)
                dve.tensor_copy(dst, ps[:, 2 + a % 2, :n]).then_inc(probs_copied, 1)

            def scale_outputs(stage, dst):
                a, n, d = ATT[stage]
                cols = slice(COLUMN[stage], COLUMN[stage] + n)
                dve.wait_ge(powed, a + n)
                link(dve.reciprocal(rec[:, cols, :], tot[:, cols, :]))
                dve.wait_ge(mixed, a + n)
                for t in range(NT):
                    dve.tensor_tensor(dst(t).rearrange("p (a b) -> p a b", b=d), bank(4 + t).rearrange("p (a b) -> p a b", b=d),
                                      rec[:, cols, t:t + 1].to_broadcast([P, n, d]), ALU.mult).then_inc(attended, 1)

            def feed_forward(layer):
                up = FIRST[f"up{layer}"]
                J0 = KF * layer

                linked = links[0]

                def low(j, r):
                    dve.wait_ge(h_hi_done, J0 + j + 1)
                    dve.tensor_tensor(h_lo[:, j, :], pt[:, r % 2, :S], h_hi[:, j, :].bitcast(F32), ALU.subtract).then_inc(h_lo_done, 1)

                def tile(i, r):
                    j = 4 * i + r
                    if layer < 2:
                        c = sc[:, r % 2, :S]
                        dve.wait_ge(conv_begun, J0 + j + 1)
                        dve.scalar_tensor_tensor(c[:, 1:S], ps[:, r, 0:S - 1], conv[:, layer, j, 1:2], c[:, 1:S], ALU.mult, ALU.add).then_inc(dve_link, 1)
                        dve.wait_ge(dve_link, linked + j + 1)
                        dve.scalar_tensor_tensor(c[:, 2:S], ps[:, r, 0:S - 2], conv[:, layer, j, 0:1], c[:, 2:S],
                                                 ALU.mult, ALU.add).then_inc(conv_done, 1)
                    if not (type(i) is int and j == 0):
                        low(j - 1, r + 3)
                    split_unit(j + up + 2, (up + 2 + r) % RAW, UNIT)
                    dve.wait_ge(glued, J0 + j + 1)
                    dve.tensor_tensor(pt[:, r % 2, :S], ps[:, r, S:2 * S], pr[:, r % 2, :S], ALU.mult).then_inc(hmul, 1)

                each_tile(dve, tile)
                low(KF - 1, KF - 1)
                links[0] += KF if layer < 2 else 0
                done[0] += KF
                units(last(f"down{layer}"))

            dve.wait_ge(mem_in[0], 16)
            norm(0, 0, 0, mem_x)
            units(1)
            turned_lo(0, 4, h_lo, h_hi, (0,))
            dve.wait_ge(mem_in[1], 16)
            norm(0, 0, 1, mem_x)
            units(2)
            turned_lo(0, 4, h_lo, h_hi, (1,))
            dve.wait_ge(x_in, 16)
            for t in range(NT):
                norm(1, 1, t, h)
            units(FIRST["even_a"])
            turned_lo(1, 4, y_lo, y_hi)
            units(FIRST["even_a"] + 1)
            dve.wait_ge(unit_used, last("mem_kv"))
            for t in range(NT):
                dve.tensor_copy(mv[:, t, :], bank(2 * t + 1)).then_inc(mv_copied, 1)
            units(FIRST["even_a"] + 2)
            dve.wait_ge(const_in, 16 * 12)
            dve.wait_ge(set_up, 4)
            for t in range(NT):
                head_sums(t, 4, P)
            for t in range(NT):
                v = heads_view(mk[:, t, :], P)
                head_scale(t, v, v, 4, P)
                head_gains(v, 4, P, 384).then_inc(mk_ready, 1)
                units(FIRST["even_a"] + 3 + t)
            dve.tensor_tensor(lb_d[:, :], lb_in[:, 0, :], lb_in[:, 1, :], ALU.subtract).then_inc(lb_sub, 1)
            units(last("even_a") + 1)
            dve.wait_ge(lb_sig, 1)
            dve.tensor_scalar(lb[:, 1, :], lb[:, 0, :], -1.0, 1.0, ALU.mult, ALU.add).then_inc(lb_done, 1)
            dve.wait_ge(unit_used, last("even_a"))
            for t in range(NT):
                x = heads_view(two_banks(4 + 2 * t)[:, :640], HD)
                o = heads_view(qk[:, t, :], HD)
                w = heads_view(rot[:, :], HD)
                cos, sin, nsin = (rope_a[:, i, t:t + 1, :].to_broadcast([P, 10, 32]) for i in range(3))
                dve.tensor_tensor(o[:, :, 0:32], x[:, :, 0:32], cos, ALU.mult)
                dve.tensor_tensor(o[:, :, 32:64], x[:, :, 32:64], cos, ALU.mult)
                dve.tensor_tensor(w[:, :, 0:32], x[:, :, 32:64], nsin, ALU.mult)
                dve.tensor_copy(va[:, t, :], two_banks(4 + 2 * t)[:, 640:768])
                link(dve.tensor_tensor(w[:, :, 32:64], x[:, :, 0:32], sin, ALU.mult))
                dve.tensor_tensor(qk[:, t, :], qk[:, t, :], rot[:, :], ALU.add).then_inc(roped, 1)
                dve.wait_ge(roped, t + 1)
                units(last("even_a") + 2 + t)
            units(last("even_qf") + 1)
            dve.wait_ge(qf_evac, 4)
            dve.wait_ge(lb_done, 1)
            for hh in range(HB):
                ins = dve.tensor_scalar(hf[:, hh, :], hf[:, hh, :], lb[:, 1, hh:hh + 1], lb[:, 0, hh:hh + 1], ALU.mult, ALU.add)
            link(ins)
            dve.tensor_scalar(whole(hk), whole(hf), -1.0, 1.0, ALU.mult, ALU.add).then_inc(f_done, 1)
            units(FIRST["even_ig"] + 2)
            dve.wait_ge(ln_done, 1)
            for hh in range(HB):
                ins = dve.tensor_tensor_scan(hc[:, hh, :], keep[:, :], hf[:, hh, :], 0.0, ALU.mult, ALU.add)
            ins.then_inc(cum_done, 1)
            dve.wait_ge(cum_done, 1)
            blocks = whole(hc).rearrange("p (n l) -> p n l", l=BLK)
            dve.tensor_tensor(whole(hf).rearrange("p (n l) -> p n l", l=BLK), blocks[:, :, BLK - 1:BLK].to_broadcast([P, HB * NBLK, BLK]),
                              blocks, ALU.subtract).then_inc(last_done, 1)
            units(FIRST["even_ig"] + 3)
            dve.wait_ge(exp_done, 2)
            dve.tensor_tensor(whole(hq), whole(hq), whole(he), ALU.mult).then_inc(dec_done, 1)
            dve.tensor_tensor(whole(hd), whole(hk), whole(hd), ALU.mult).then_inc(dec_done, 1)
            units(FIRST["even_ig"] + 4)
            dve.wait_ge(exp3_done, 1)
            dve.tensor_tensor(whole(hc), whole(hk), whole(hf), ALU.mult).then_inc(dec_done, 1)
            units(last("even_ig") + 1)
            dve.wait_ge(unit_used, last("even_ig"))
            for t in range(NT):
                dve.tensor_copy(hv[:, t, :], bank(4 + 2 * t)).then_inc(hv_evac, 1)
            units(last("even_ig") + 2)
            mask = block_causal[:, :].rearrange("p (a b) -> p a b", a=1).to_broadcast([P, HB, P])
            for t in range(NT):
                dve.wait_ge(st_made, t + 1)
                dve.copy_predicated(s_t[:, t, :, :], mask, split4(bank(3 + t))).then_inc(st_evac, 1)
            decay = whole(he).rearrange("p (h n l) -> p h n l", h=HB, l=BLK)
            dve.wait_ge(dec_done, 3)
            for b in range(NBLK - 1):
                dve.wait_ge(kv_made, b + 1)
                kv = split4(bank(5 + b % 3))
                if b == 0:
                    dve.tensor_copy(state[0], kv).then_inc(stated, 1)
                    continue
                dve.wait_ge(stated, b)
                for hh in range(HB):
                    ins = dve.scalar_tensor_tensor(state[b][:, hh, :], state[b - 1][:, hh, :], decay[:, hh, b, BLK - 1:BLK],
                                                   kv[:, hh, :], ALU.mult, ALU.add)
                ins.then_inc(stated, 1)
            dve.wait_ge(gated, 2)
            for t in range(NT):
                head_sums(2 + t, 4, P)
            dve.wait_ge(head_sum, 4)
            scores_max("a", 0)
            for t in range(NT):
                o = heads_view(xhat[:, t, 512:1024], P)
                head_scale(2 + t, o, split4(bank(4 + t)), 4, P)
                dve.tensor_tensor(xhat[:, t, 512:1024], xhat[:, t, 512:1024], hg[:, t, :], ALU.mult).then_inc(hgrn_out, 1)
                if t == 0:
                    scores_max("a", 1)
            dve.wait_ge(hgrn_out, 2)
            for i in range(2, 10):
                if i < 8:
                    scores_max("a", i)
                if i == 8:
                    dve.wait_ge(maxed, 8)
                    dve.tensor_tensor(snk[:, :, :], neg[:, 0:8, :], rows_in[:, 0:8].rearrange("p (a b) -> p a b", b=1).to_broadcast([P, 8, 2]),
                                      ALU.add).then_inc(dve_sink, 1)
                probs_copy("a", i - 2)
            dve.wait_ge(act_sink, 1)
            dve.wait_ge(powed, 8)
            link(dve.tensor_tensor(tot[:, 0:8, :], tot[:, 0:8, :], esnk[:, :, :], ALU.add))
            scale_outputs("a", lambda t: xhat[:, t, 0:512])
            turned_lo(2, 4, y_lo, y_hi)
            units(last("even_out"))
            norms_between(2, 0, 0, "even_out", 3, 4, 2)
            feed_forward(0)
            norms_between(4, 1, 4, "down0", 4, 0, 3)

            units(last("odd_k") + 1)
            dve.wait_ge(unit_used, last("odd_k"))
            dve.tensor_copy(k1[:, 1, :], two_banks(2)).then_inc(k_evac, 1)
            units(last("odd_k") + 2)
            for b in range(2, 4):
                dve.wait_ge(qk_turned, 4 + b + 1)
                dve.tensor_copy(token_half(k1_t, b % 2, b // 2), split4(bank(b))).then_inc(k_copied, 1)
            units(last("odd_v"))
            for hh in range(16):
                scores_max("c", hh)
                if hh >= 1:
                    probs_copy("c", hh - 1)
                if hh == 8:
                    dve.wait_ge(unit_used, last("odd_v"))
                    dve.tensor_copy(v1[:, 1, :], two_banks(6)).then_inc(v_evac, 1)
                if hh >= 4:
                    split_part(4, hh % 4)
            probs_copy("c", 15)
            dve.wait_ge(turned, 20)
            link(dve.reciprocal(rec[:, 0:16, :], tot[:, 0:16, :]))
            for t in range(NT):
                dve.wait_ge(*((first_mixed, 1) if t == 0 else (mixed, 24)))
                dve.tensor_tensor(xhat[:, t, :].rearrange("p (a b) -> p a b", b=HD), two_banks(4 + 2 * t).rearrange("p (a b) -> p a b", b=HD),
                                  rec[:, 0:16, t:t + 1].to_broadcast([P, 16, HD]), ALU.mult).then_inc(attended, 1)
            turned_lo(5, 0, y_lo, y_hi)
            units(last("odd_out"))
            norms_between(6, 2, 4, "odd_out", 6, 4, 4)
            feed_forward(1)
            norms_between(8, 3, 4, "down1", 7, 0, 5)

            units(last("moba_qk") + 1)
            dve.wait_ge(unit_used, last("moba_qk"))
            dve.tensor_copy(qkm[:, 1, :], two_banks(6)).then_inc(m_evac, 1)
            units(last("moba_qk") + 2)
            for t in range(NT):
                head_sums(4 + t, 16, HD)
            n = last("moba_qk") + 3
            units(n)
            for t in range(NT):
                v = heads_view(qkm[:, t, :], HD)
                head_scale(4 + t, v, v, 16, HD)
                head_gains(v[:, 0:8], 8, HD, 0)
                link(head_gains(v[:, 8:16], 8, HD, 64))
                n += 1
                units(min(n, last("both_v") + 1))
                w = [heads_view(pt[:, 0, 128 * i:128 * i + 128], 8) for i in range(4)]
                cos, sin, nsin = (rope_m[:, i, t:t + 1, :].to_broadcast([P, 16, 8]) for i in range(3))
                x1, x2 = v[:, :, 0:8], v[:, :, 8:16]
                dve.tensor_tensor(w[0], x1, cos, ALU.mult)
                dve.tensor_tensor(w[1], x2, nsin, ALU.mult)
                dve.tensor_tensor(w[2], x2, cos, ALU.mult)
                link(dve.tensor_tensor(w[3], x1, sin, ALU.mult))
                dve.tensor_tensor(x1, w[0], w[1], ALU.add)
                dve.tensor_tensor(x2, w[2], w[3], ALU.add).then_inc(m_ready, 1)
                dve.wait_ge(m_ready, t + 1)
            units(last("both_v") + 1)
            dve.wait_ge(unit_used, last("both_v"))
            dve.tensor_copy(v2[:, 1, :], two_banks(2)).then_inc(v2_evac, 1)
            units(last("fox_qk") + 1)
            dve.wait_ge(unit_used, last("fox_qk"))
            dve.tensor_copy(qkf[:, 1, :], two_banks(6)).then_inc(f_evac, 1)
            units(last("fox_qk") + 2)
            for t in range(NT):
                head_sums(6 + t, 16, HD)
            units(last("fox_qk") + 3)
            for t in range(NT):
                v = heads_view(qkf[:, t, :], HD)
                head_scale(6 + t, v, v, 16, HD)
                head_gains(v[:, 0:8], 8, HD, 128)
                head_gains(v[:, 8:16], 8, HD, 192).then_inc(f_ready, 1)
                units(last("mem_q") + t)
            units(last("mem_q") + 1)
            dve.wait_ge(unit_used, last("mem_q"))
            for t in range(NT):
                dve.tensor_tensor(fz[:, 0, t, :], ps[:, 2 * t, 0:8], rows_in[:, 8:16], ALU.add).then_inc(z_done, 1)
            dve.wait_ge(z_done, 2)
            dve.scalar_tensor_tensor(fz[:, 1, :, :], fz[:, 0, :, :], -1.0, fz[:, 0, :, :], ALU.mult, ALU.max).then_inc(forget, 1)
            link(dve.tensor_scalar(fz[:, 4, :, :], fz[:, 0, :, :], -1.0, 0.0, ALU.mult, ALU.max))
            units(last("mem_q") + 2)
            for t in range(NT):
                head_sums(8 + t, 4, P)
            for t in range(NT):
                v = heads_view(qc[:, t, :], P)
                head_scale(8 + t, v, v, 4, P)
                head_gains(v, 4, P, 256).then_inc(c_ready, 1)
            dve.wait_ge(forget_l, 1)
            for c in (0, 64):
                ins = dve.tensor_tensor(nlf[:, :, c:c + 8], fz[:, 4, :, :], fz[:, 3, :, :], ALU.add)
            ins.then_inc(nlf_ready, 1)
            units(FIRST["gates"] + 3)
            dve.wait_ge(heads_turned, 11)
            dve.tensor_tensor_scan(ncum[:, :], ones[:, :], ps[:, 4, :S], 0.0, ALU.mult, ALU.add).then_inc(ncum_done, 1)
            for k in range(10):
                now = third_heads(k)
                for stage, hh in now:
                    scores_max(stage, hh)
                if k == 4:
                    scale_outputs("m", lambda t: qkm[:, t, 0:512])
                if k == 8:
                    scale_outputs("f", lambda t: qkf[:, t, 0:512])
                units(FIRST["gates"] + k + 4)
                for stage, hh in now:
                    probs_copy(stage, hh)
            scale_outputs("x", lambda t: qkm[:, t, 512:1024])
            for b in range(6):
                dve.wait_ge(br_hi, b + 1)
                dve.tensor_tensor(branch_y(1, b // 2, b % 2), split4(bank(b)), branch_y(0, b // 2, b % 2).bitcast(F32),
                                  ALU.subtract).then_inc(br_lo, 1)
            def merged_low(c):
                dve.wait_ge(merged_hi, c + 1)
                dve.tensor_tensor(h_lo[:, 4 * c:4 * c + 4, :], m_sum[:, 4 * c:4 * c + 4, :], h_hi[:, 4 * c:4 * c + 4, :].bitcast(F32),
                                  ALU.subtract).then_inc(merged_lo, 1)

            for u in range(6):
                b, c = u // 2, u % 2
                units(FIRST["branches"] + u + 2)
                if u == 5:
                    merged_low(0)
                dve.wait_ge(unit_used, FIRST["branches"] + u + 1)
                dve.wait_ge(gate_sig, b + 1)
                src = two_banks(2 * c)
                g = gate[:, 8 * b + 4 * c:8 * b + 4 * c + 4, :].rearrange("p a b -> p (a b)")
                m = m_sum[:, 4 * c:4 * c + 4, :].rearrange("p a b -> p (a b)")
                if b == 0:
                    dve.tensor_tensor(m, src, g, ALU.mult).then_inc(br_used, 1)
                else:
                    dve.tensor_tensor(g, src, g, ALU.mult).then_inc(br_used, 1)
                    dve.wait_ge(br_used, u + 1)
                    dve.tensor_tensor(m, m, g, ALU.add).then_inc(br_sum, 1)
            units(FIRST["merge_out"] + 2)
            merged_low(1)
            units(last("merge_out"))
            add_residual("merge_out", 4, 0)
            weigh(10, 0, [h[:, 0, 0:512], h[:, 0, 512:D]])
            units(last("merge_out") + 1)
            add_residual("merge_out", 4, 1)
            scale(10, 0)
            weigh(10, 1, [h[:, 1, 0:512], h[:, 1, 512:D]])
            turned_lo(8, 4, y_lo, y_hi, (0,))
            scale(10, 1)
            turned_lo(8, 4, y_lo, y_hi, (1,))
            units(last("merge_out") + 2)
            feed_forward(2)
            for t in range(NT):
                add_residual("down2", 4, t)
            assert done[0] == UNITS


_OUT = (1, S, D)


def kernel(**inputs):
    import concourse.bacc as bacc
    from concourse.bass_utils import run_bass_kernel_spmd

    nc = bacc.Bacc("TRN2", target_bir_lowering=False, num_devices=1)
    arrays = {**lay_out({k: np.asarray(v) for k, v in inputs.items()}), **constants()}
    arrays = {k: np.ascontiguousarray(v) for k, v in arrays.items()}
    dram = {k: nc.dram_tensor(f"in_{k}", v.shape, mybir.dt.from_np(v.dtype), kind="ExternalInput").ap() for k, v in arrays.items()}
    out = nc.dram_tensor("out", (S, D), F32, kind="ExternalOutput").ap()
    build(nc, dram, out)
    got = run_bass_kernel_spmd(nc, [{f"in_{k}": v for k, v in arrays.items()}], core_ids=[0])
    return got.results[0]["out"].reshape(_OUT)
```
